# Optimizing a Trainium2 kernel written in Bass

```python
import jax, jax.numpy as jnp
from jax import lax
import numpy as np

D_MODEL = 2048
BATCH = 1
SEQ = 512
DEPTH = 1

CHUNK = 64
EPS = 1e-6
CONV_CH = 1024
CONV_GROUPS = 8
CONV_WIDTH = 31
MLA_HEADS = 8
QK_NOPE = 128
QK_ROPE = 64
QK_HEAD = QK_NOPE + QK_ROPE
V_HEAD = 128
Q_LORA = 768
KV_LORA = 512
ROPE_THETA = 10000.0
Q_BLOCK = 128
MIX_WIDTH = CONV_CH + MLA_HEADS * V_HEAD
IN_COLS = 2 * CONV_CH + Q_LORA + KV_LORA + QK_ROPE
PEER_HEADS = 8
N_KEYS = 128
N_EXPERTS = N_KEYS * N_KEYS
PEER_TOPK = 16
PEER_QDIM = 256
PEER_HALF = PEER_QDIM // 2
TOKEN_BLOCK = 128

kernel_name = "hybrid_conv_mla_peer_adaln_block"

def rmsnorm(x, g):
    xf = x.astype(jnp.float32)
    y = xf * lax.rsqrt(jnp.mean(xf * xf, axis=-1, keepdims=True) + EPS)
    return (y * g.astype(jnp.float32)).astype(x.dtype)

def layernorm(x, g, b):
    xf = x.astype(jnp.float32)
    mu = jnp.mean(xf, axis=-1, keepdims=True)
    var = jnp.mean(jnp.square(xf - mu), axis=-1, keepdims=True)
    y = (xf - mu) * lax.rsqrt(var + EPS)
    return (y * g.astype(jnp.float32) + b.astype(jnp.float32)).astype(x.dtype)

def apply_rope(x, cos, sin):
    x1, x2 = jnp.split(x.astype(jnp.float32), 2, axis=-1)
    out = jnp.concatenate([x1 * cos - x2 * sin, x2 * cos + x1 * sin], axis=-1)
    return out.astype(x.dtype)

def conv_module(a, dw_w, dw_b, ln_g, ln_b):
    val, gate = jnp.split(a, 2, axis=-1)
    h = val * jax.nn.sigmoid(gate)
    h = lax.conv_general_dilated(
        h, dw_w[:, None, :], window_strides=(1,), padding=[(CONV_WIDTH - 1, 0)],
        dimension_numbers=("NWC", "WIO", "NWC"), feature_group_count=CONV_CH) + dw_b
    h = layernorm(h, ln_g, ln_b)
    return jax.nn.silu(h)

def chunk_causal_attention(q, k, v):
    B, H, S, Dk = q.shape
    nb = S // Q_BLOCK
    qb = q.reshape(B, H, nb, Q_BLOCK, Dk).transpose(2, 0, 1, 3, 4)
    k_chunk = jnp.arange(S) // CHUNK
    scale = QK_HEAD ** -0.5

    def one_block(args):
        qi, bi = args
        s = jnp.einsum("bhqd,bhkd->bhqk", qi, k).astype(jnp.float32) * scale
        q_chunk = (bi * Q_BLOCK + jnp.arange(Q_BLOCK)) // CHUNK
        mask = k_chunk[None, :] <= q_chunk[:, None]
        s = jnp.where(mask, s, -jnp.inf)
        p = jax.nn.softmax(s, axis=-1).astype(v.dtype)
        return jnp.einsum("bhqk,bhkd->bhqd", p, v)

    out = lax.map(one_block, (qb, jnp.arange(nb)))
    return out.transpose(1, 2, 0, 3, 4).reshape(B, H, S, v.shape[-1])

def mla(q_lat, kv_lat, k_rope, positions, q_a_norm_g, w_uq, kv_a_norm_g, w_ukv, q_norm_g, k_norm_g):
    B, S, _ = q_lat.shape
    q = (rmsnorm(q_lat, q_a_norm_g) @ w_uq).reshape(B, S, MLA_HEADS, QK_HEAD)
    kv = (rmsnorm(kv_lat, kv_a_norm_g) @ w_ukv).reshape(B, S, MLA_HEADS, QK_NOPE + V_HEAD)
    k_nope, v = kv[..., :QK_NOPE], kv[..., QK_NOPE:]
    k_r = jnp.broadcast_to(k_rope[:, :, None, :], (B, S, MLA_HEADS, QK_ROPE))
    k = jnp.concatenate([k_nope, k_r], axis=-1)
    q = rmsnorm(q, q_norm_g).transpose(0, 2, 1, 3)
    k = rmsnorm(k, k_norm_g).transpose(0, 2, 1, 3)
    v = v.transpose(0, 2, 1, 3)
    inv_freq = ROPE_THETA ** (-jnp.arange(0, QK_ROPE, 2, dtype=jnp.float32) / QK_ROPE)
    ang = positions.astype(jnp.float32)[..., None] * inv_freq
    cos, sin = jnp.cos(ang)[:, None], jnp.sin(ang)[:, None]
    q = jnp.concatenate([q[..., :QK_NOPE], apply_rope(q[..., QK_NOPE:], cos, sin)], axis=-1)
    k = jnp.concatenate([k[..., :QK_NOPE], apply_rope(k[..., QK_NOPE:], cos, sin)], axis=-1)
    o = chunk_causal_attention(q, k, v)
    return o.transpose(0, 2, 1, 3).reshape(B, S, MLA_HEADS * V_HEAD)

def peer(h, wq, k1, k2, u, v):
    B, S, D = h.shape
    T = B * S
    xt = h.reshape(T, D)
    q = (xt @ wq).reshape(T, PEER_HEADS, 2, PEER_HALF)
    s1 = jnp.einsum("thd,hnd->thn", q[:, :, 0], k1).astype(jnp.float32)
    s2 = jnp.einsum("thd,hnd->thn", q[:, :, 1], k2).astype(jnp.float32)
    v1, i1 = lax.top_k(s1, PEER_TOPK)
    v2, i2 = lax.top_k(s2, PEER_TOPK)
    cand = (v1[..., :, None] + v2[..., None, :]).reshape(T, PEER_HEADS, PEER_TOPK * PEER_TOPK)
    best, flat = lax.top_k(cand, PEER_TOPK)
    e1 = jnp.take_along_axis(i1, flat // PEER_TOPK, axis=-1)
    e2 = jnp.take_along_axis(i2, flat % PEER_TOPK, axis=-1)
    experts = e1 * N_KEYS + e2
    gates = jax.nn.softmax(best, axis=-1).astype(h.dtype)
    nb = T // TOKEN_BLOCK

    def one_block(args):
        xb, eb, gb = args
        a = jnp.einsum("td,thkd->thk", xb, u[eb])
        act = gb * jax.nn.gelu(a)
        return jnp.einsum("thk,thkd->td", act, v[eb])

    y = lax.map(one_block, (xt.reshape(nb, TOKEN_BLOCK, D),
                            experts.reshape(nb, TOKEN_BLOCK, PEER_HEADS, PEER_TOPK),
                            gates.reshape(nb, TOKEN_BLOCK, PEER_HEADS, PEER_TOPK)))
    return y.reshape(B, S, D)

def setup_inputs(seed: int = 0) -> dict:
    key = jax.random.key(seed)
    ks = jax.random.split(key, 24)
    L, D = DEPTH, D_MODEL

    def nrm(k, shape, scale):
        return jax.random.normal(k, shape, dtype=jnp.float32) * scale

    positions = (jax.random.randint(ks[2], (BATCH, 1), 0, 16) * CHUNK
                 + jnp.arange(SEQ)[None, :]).astype(jnp.int32)
    return {
        "x": nrm(ks[0], (BATCH, SEQ, D), 1.0),
        "c": nrm(ks[1], (BATCH, D), 1.0),
        "positions": positions,
        "w_ada": nrm(ks[3], (L, D, 6 * D), 0.5 * D ** -0.5),
        "b_ada": nrm(ks[4], (L, 6 * D), 0.02),
        "norm1_g": 1.0 + nrm(ks[5], (L, D), 0.02),
        "w_in": nrm(ks[6], (L, D, IN_COLS), D ** -0.5),
        "conv_dw_w": nrm(ks[7], (L, CONV_WIDTH, CONV_CH), CONV_WIDTH ** -0.5),
        "conv_dw_b": nrm(ks[8], (L, CONV_CH), 0.02),
        "conv_ln_g": 1.0 + nrm(ks[9], (L, CONV_CH), 0.02),
        "conv_ln_b": nrm(ks[10], (L, CONV_CH), 0.02),
        "q_a_norm_g": 1.0 + nrm(ks[11], (L, Q_LORA), 0.02),
        "w_uq": nrm(ks[12], (L, Q_LORA, MLA_HEADS * QK_HEAD), Q_LORA ** -0.5),
        "kv_a_norm_g": 1.0 + nrm(ks[13], (L, KV_LORA), 0.02),
        "w_ukv": nrm(ks[14], (L, KV_LORA, MLA_HEADS * (QK_NOPE + V_HEAD)), KV_LORA ** -0.5),
        "q_norm_g": 1.0 + nrm(ks[15], (L, QK_HEAD), 0.02),
        "k_norm_g": 1.0 + nrm(ks[16], (L, QK_HEAD), 0.02),
        "w_out": nrm(ks[17], (L, MIX_WIDTH, D), MIX_WIDTH ** -0.5),
        "norm2_g": 1.0 + nrm(ks[18], (L, D), 0.02),
        "peer_wq": nrm(ks[19], (L, D, PEER_HEADS * PEER_QDIM), D ** -0.5),
        "peer_k1": nrm(ks[20], (L, PEER_HEADS, N_KEYS, PEER_HALF), PEER_HALF ** -0.5),
        "peer_k2": nrm(ks[21], (L, PEER_HEADS, N_KEYS, PEER_HALF), PEER_HALF ** -0.5),
        "peer_u": nrm(ks[22], (L, N_EXPERTS, D), D ** -0.5),
        "peer_v": nrm(ks[23], (L, N_EXPERTS, D), 0.3),
    }

def reference(x, c, positions, w_ada, b_ada, norm1_g, w_in, conv_dw_w, conv_dw_b, conv_ln_g,
              conv_ln_b, q_a_norm_g, w_uq, kv_a_norm_g, w_ukv, q_norm_g, k_norm_g, w_out,
              norm2_g, peer_wq, peer_k1, peer_k2, peer_u, peer_v):
    c_act = jax.nn.silu(c)
    for l in range(DEPTH):
        mod = c_act @ w_ada[l] + b_ada[l]
        shift1, scale1, gate1, shift2, scale2, gate2 = [m[:, None, :] for m in jnp.split(mod, 6, axis=-1)]

        h = rmsnorm(x, norm1_g[l]) * (1.0 + scale1) + shift1
        a = h @ w_in[l]
        o1 = 2 * CONV_CH
        o2 = o1 + Q_LORA
        o3 = o2 + KV_LORA
        conv_out = conv_module(a[..., :o1], conv_dw_w[l], conv_dw_b[l], conv_ln_g[l], conv_ln_b[l])
        attn_out = mla(a[..., o1:o2], a[..., o2:o3], a[..., o3:], positions,
                       q_a_norm_g[l], w_uq[l], kv_a_norm_g[l], w_ukv[l], q_norm_g[l], k_norm_g[l])
        mix = jnp.concatenate([conv_out, attn_out], axis=-1) @ w_out[l]
        x = x + gate1 * mix

        h2 = rmsnorm(x, norm2_g[l]) * (1.0 + scale2) + shift2
        x = x + gate2 * peer(h2, peer_wq[l], peer_k1[l], peer_k2[l], peer_u[l], peer_v[l])
    return x


_drawn_inputs = setup_inputs


def setup_inputs(seed=0):
    import zlib

    import numpy as np

    out = dict(_drawn_inputs(seed))
    spreads = {}
    factors = {'b_ada': 3.904,
     'norm1_g': 8.0,
     'conv_dw_b': 8.0,
     'conv_ln_g': 22.134,
     'conv_ln_b': 22.782,
     'q_a_norm_g': 8.0,
     'w_uq': 2.735,
     'kv_a_norm_g': 8.0,
     'q_norm_g': 8.0,
     'k_norm_g': 8.0,
     'norm2_g': 21.439}
    for name, (base, spread) in spreads.items():
        noise = np.random.default_rng([zlib.crc32(name.encode()), seed]).standard_normal(out[name].shape)
        drawn = base * np.exp(spread * noise) if base else spread * noise
        out[name] = __import__('jax').numpy.asarray(drawn.astype(out[name].dtype))
    for name, factor in factors.items():
        out[name] = (out[name] * factor).astype(out[name].dtype)
    return out
```

```python
from contextlib import ExitStack

import concourse.bass as bass
from concourse import mybir

F32 = mybir.dt.float32
F32R = mybir.dt.float32r
U32 = mybir.dt.uint32
I32 = mybir.dt.int32
ALU = mybir.AluOpType
ACT = mybir.ActivationFunctionType
AX_X = mybir.AxisListType.X

P = 128
T = 512
D = 2048
KD = D // P
TB = T // P
EPS = 1e-6
CONV_CH, CONV_W = 1024, 31
NC_T = CONV_CH // P
HEADS, NOPE, ROPE, VH = 8, 128, 64, 128
Q_LORA, KV_LORA = 768, 512
KQ, KKV = Q_LORA // P, KV_LORA // P
NLAT = KQ + KKV
SCALE = float(NOPE + ROPE) ** -0.5
PH_, TOPK, NKEY = 8, 16, 128
NEG = -3.0e38
CH = KD * P

J_KR, J_LAT = 0, 1
J_CONV = J_LAT + NLAT
J_QR = J_CONV + 2 * NC_T
J_HEAD = J_QR + 2
J_OUT = J_HEAD + HEADS
J_WQ = J_OUT + KD
J_U = J_WQ + KD
J_V = J_U + NKEY
N_JOBS = J_V + NKEY

_cols = [("g1", KD), ("g2", KD), ("conv_b", NC_T), ("ln_g", NC_T), ("ln_b", NC_T), ("conv_w", NC_T * CONV_W),
         ("qa_g", KQ), ("kva_g", KKV), ("qn_g", 1), ("qr_g", 1), ("kn_g", 1), ("kr_g", 1),
         ("b_ada", 6 * KD), ("inv_freq", 1)]
COL, _n = {}, 0
for _name, _w in _cols:
    COL[_name] = (_n, _n + _w)
    _n += _w
NPRM = _n


LEAD, DMA_LEAD = 1, 16


class Tally:

    def __init__(self, eng, sem):
        self.eng, self.sem, self.base, self.turn, self.k = eng, sem, 0, None, 0

    def open(self, turn, per_turn):
        self.base += self.k
        self.turn, self.per, self.k = turn, per_turn, 0

    def close(self, turns):
        assert self.k == self.per, (self.k, self.per)
        self.base += self.per * turns
        self.turn, self.k = None, 0

    def mark(self, ins):
        ins.then_inc(self.sem, 1)
        self.k += 1
        return self.k

    def after(self, k):
        v = self.base + k
        self.eng.wait_ge(self.sem, v if self.turn is None else self.turn * self.per + v)

    def step(self, ins):
        self.after(self.mark(ins))


def build(nc, x_d, c_d, pos_d, prm_d, wada_d, win_d, wqr_d, whd_d, wout_d, wwq_d, keys_d, u_d, v_d, out_d):
    gelu_d = nc.dram_tensor("gelu_scratch", [NKEY, P, T], F32).ap()
    gate_d = nc.dram_tensor("gate_scratch", [8, P, NKEY, 64], F32).ap()
    x1_d = nc.dram_tensor("x1_scratch", [P, KD, T], F32).ap()

    with ExitStack() as ctx:
        def at(name, kb, shape, dt=F32):
            return nc.alloc_sbuf_tensor_at(name, shape, dt, offset=1152 + int(kb * 1024))

        sems = {}

        def sem(name):
            if name not in sems:
                sems[name] = ctx.enter_context(nc.semaphore(name))
            return sems[name]

        bank = [ctx.enter_context(nc.psum_tensor(f"bank{i}", [P, T], F32)) for i in range(8)]

        act_hi = at("act_hi", 0, [P, KD, T], F32R)
        act_lo = at("act_lo", 32, [P, KD, T], F32R)
        att_o = at("att_o", 20, [P, HEADS, T])
        sq_qr = at("sq_qr", 36, [P, 4, T])
        w_raw = [at(f"w_raw{s}", 64 + 8 * s, [P, CH]) for s in range(2)]
        w_hi = [at(f"w_hi{s}", 80 + 8 * s, [P, CH], F32R) for s in range(2)]
        w_lo = [at(f"w_lo{s}", 96 + 8 * s, [P, CH], F32R) for s in range(2)]
        X = at("X", 112, [P, KD, T])
        conv_o = at("conv_o", 112, [P, NC_T, T])
        sig = at("sig", 128, [P, T])
        glu = at("glu", 130, [P, CONV_W - 1 + T])
        tap_a = at("tap_a", 133, [P, T])
        tap_b = at("tap_b", 135, [P, T])
        conv_ws = at("conv_ws", 137, [P, CONV_W + 1])
        kr_rot = at("kr_rot", 138, [P, T])
        kr_sq = at("kr_sq", 140, [P, T])
        swapped = at("swapped", 142, [P, T])
        ada_w = [at(f"ada_w{s}", 144 + 8 * s, [P, D]) for s in range(4)]
        lat = at("lat", 160, [P, 1 + NLAT, T])
        c_all = at("c_all", 182, [P, D])
        sq = [at(f"sq{s}", 190 + 2 * s, [P, T]) for s in range(2)]
        qr_rot = at("qr_rot", 194, [P, 4, T])
        cos_t = at("cos_t", 204, [P, T])
        sin_t = at("sin_t", 206, [P, T])
        root = at("root", 208, [P, T])
        rstd = at("rstd", 210, [P, T])
        q_n = [at("q_n0", 128, [P, T]), at("q_n1", 190, [P, T])]
        k_n = [at("k_n0", 130, [P, T]), at("k_n1", 192, [P, T])]
        q_r = [at("q_r0", 132, [P, T]), at("q_r1", 202, [P, T])]
        k_r = [at("k_r0", 134, [P, T]), at("k_r1", 180, [P, T])]
        v_s = [at(f"v_s{s}", 160 + 2 * s, [P, T]) for s in range(2)]
        prob = [at(f"prob{s}", 164 + 2 * s, [P, T]) for s in range(2)]
        prob_t = at("prob_t", 168, [P, TB, T])
        sq_q = at("sq_q", 176, [P, T])
        sq_k = at("sq_k", 178, [P, T])
        flat_all = at("flat_all", 112, [P, TB, PH_, TOPK], U32)
        i1_all = at("i1_all", 114, [P, TB, PH_, TOPK], U32)
        i2_all = at("i2_all", 116, [P, TB, PH_, TOPK], U32)
        best_all = at("best_all", 118, [P, TB, PH_, TOPK])
        pick = at("pick", 120, [P, PH_, TOPK, TOPK])
        e1_t = at("e1_t", 128, [P, TB, P])
        e2_t = at("e2_t", 130, [P, TB, P])
        gate_t = at("gate_t", 132, [P, TB, P])
        part = at("part", 134, [P, P], U32)
        shifted = at("shifted", 134.5, [P, PH_, TOPK])
        expd = at("expd", 135, [P, PH_, TOPK])
        esum = at("esum", 135.5, [P, PH_])
        ersum = at("ersum", 135.75, [P, PH_])
        q_t = [at(f"q_t{s}", 144 + 2 * s, [P, T]) for s in range(2)]
        val = [at(f"val{s}", 148 + .25 * s, [P, TB, TOPK]) for s in range(2)]
        idx = [at(f"idx{s}", 148.5 + .25 * s, [P, TB, TOPK], U32) for s in range(2)]
        best = at("best", 149, [P, TB, TOPK])
        flat = at("flat", 149.25, [P, TB, TOPK], U32)
        s_left = [at(f"s_left{s}", 150 + .5 * s, [P, NKEY]) for s in range(2)]
        cand = at("cand", 151, [P, TOPK * TOPK])
        c_left = at("c_left", 152, [P, TOPK * TOPK])
        keys = at("keys", 160, [P, PH_, 2, NKEY])
        g_chunk = [at(f"g_chunk{s}", 112 + 32 * s, [P, NKEY, 64]) for s in range(2)]
        hot2 = at("hot2", 176, [P, 16, P], F32R)
        hot1h = at("hot1h", 184, [P, 16, P], F32R)
        hot1l = at("hot1l", 192, [P, 16, P], F32R)
        gelu_s = [at(f"gelu_s{s}", 200 + 2 * s, [P, T]) for s in range(2)]
        e1_c = at("e1_c", 204, [P, T])
        e2_c = at("e2_c", 206, [P, T])
        gate_h = at("gate_h", 208, [P, T], F32R)
        gate_l = at("gate_l", 210, [P, T])
        wt_hi = [at(f"wt_hi{s}", 112 + 4 * s, [P, 2, T], F32R) for s in range(2)]
        wt_lo = [at(f"wt_lo{s}", 120 + 4 * s, [P, 2, T], F32R) for s in range(2)]
        wt = [at(f"wt{s}", 128 + 4 * s, [P, 2, T]) for s in range(2)]
        gelu_l = [at(f"gelu_l{s}", 136 + 4 * s, [P, 2, T]) for s in range(2)]
        gate_l2 = [at(f"gate_l2{s}", 144 + 4 * s, [P, 8, 2, 64]) for s in range(2)]
        x1_s = at("x1_s", 152, [P, 8, T])
        out_s = at("out_s", 168, [P, 8, T])
        prm = at("prm", 212, [P, NPRM])
        mod_raw = at("mod_raw", 214, [P, 6 * KD])
        mod = at("mod", 214.5, [P, 6 * KD])
        amp = at("amp", 215, [P, 2, KD])
        ones = at("ones", 215.25, [P, P])
        half = [at(f"half{s}", 215.75 + .5 * s, [P, P]) for s in range(2)]
        iota_i = at("iota_i", 216.75, [P, P], I32)
        iota_f = at("iota_f", 217.25, [P, P])
        ident = at("ident", 217.75, [P, P])
        tiny = at("tiny", 218.25, [P, 16])
        pos_i = at("pos_i", 219, [P, T], I32)
        eps_c, pidx, pidx_i = tiny[:, 0:1], tiny[:, 1:2], at("pidx_i", 218.5, [P, 1], I32)
        mx = [tiny[:, 2 + s:3 + s] for s in range(2)]
        nmx = [tiny[:, 4 + s:5 + s] for s in range(2)]
        rsum = [tiny[:, 6 + s:7 + s] for s in range(2)]
        rrec = [tiny[:, 8 + s:9 + s] for s in range(2)]
        hb = [bank[5], bank[6]]

        def pcol(name, i=0, n=1):
            a = COL[name][0] + i
            return prm[:, a:a + n]

        w_loaded = [sem(f"w_loaded{s}") for s in range(2)]
        hi_done, lo_done, pe_jobs = sem("hi_done"), sem("lo_done"), sem("pe_jobs")
        ada_loaded = [sem(f"ada_loaded{s}") for s in range(4)]
        ada_used = sem("ada_used")
        x_loaded, small_loaded, c_loaded, c_ready = sem("x_loaded"), sem("small_loaded"), sem("c_loaded"), sem("c_ready")
        const_ready, pool_chain = sem("const_ready"), sem("pool_chain")
        sq_ready, sq_used, sum_ready, root_ready, rstd_ready = (sem(n) for n in ("sq_ready", "sq_used", "sum_ready", "root_ready", "rstd_ready"))
        scaled, shifted_s, h_hi, h_lo = sem("scaled"), sem("shifted_s"), sem("h_hi"), sem("h_lo")
        angle_ready, trig_ready = sem("angle_ready"), sem("trig_ready")
        bank_used = [sem(f"bank_used{s}") for s in range(2)]
        lat_scaled, lat_hi, lat_lo = sem("lat_scaled"), sem("lat_hi"), sem("lat_lo")
        sig_ready, val_used, conv_done = sem("sig_ready"), sem("val_used"), sem("conv_done")
        rope_g, rope_sw, rope_done, rope_sq, qr_ready = (sem(n) for n in ("rope_g", "rope_sw", "rope_done", "rope_sq", "qr_ready"))
        q_ready, k_ready, q_used, k_used, v_copied = (sem(n) for n in ("q_ready", "k_ready", "q_used", "k_used", "v_copied"))
        sqn_ready, ssq_ready, hroot_ready, hrstd_ready, qk_ready = (sem(n) for n in ("sqn_ready", "ssq_ready", "hroot_ready", "hrstd_ready", "qk_ready"))
        score_ready, max_ready, exp_ready, prob_ready, tr_ready, pt_ready, pv_ready, att_ready = (
            sem(n) for n in ("score_ready", "max_ready", "exp_ready", "prob_ready", "tr_ready", "pt_ready", "pv_ready", "att_ready"))
        mean_sum, mean_ready, centred, var_sum, ln_scaled, ln_silu, mix_hi, mix_lo = (
            sem(n) for n in ("mean_sum", "mean_ready", "centred", "var_sum", "ln_scaled", "ln_silu", "mix_hi", "mix_lo"))
        x2_loaded, x1_stored, keys_loaded = sem("x2_loaded"), sem("x1_stored"), sem("keys_loaded")
        qt_ready, sc_ready, sc_used = sem("qt_ready"), sem("sc_ready"), sem("sc_used")
        gmax_ready, gexp_ready, tables_ready, tabt_ready, tabt_used = (sem(n) for n in ("gmax_ready", "gexp_ready", "tables_ready", "tabt_ready", "tabt_used"))
        gelu_ready = sem("gelu_ready")
        gelu_stored = [sem(f"gelu_stored{s}") for s in range(2)]
        hot_ready = [sem(f"hot_ready{s}") for s in range(4)]
        hot_used = [sem(f"hot_used{s}") for s in range(4)]
        g_copied = [sem(f"g_copied{s}") for s in range(2)]
        g_stored = [sem(f"g_stored{s}") for s in range(2)]
        wt_loaded = [sem(f"wt_loaded{s}") for s in range(2)]
        wt_ready = [sem(f"wt_ready{s}") for s in range(2)]
        wth_ready = [sem(f"wth_ready{s}") for s in range(2)]
        wtl_ready = [sem(f"wtl_ready{s}") for s in range(2)]
        x1_loaded, y_ready, out_stored = sem("x1_loaded"), sem("y_ready"), sem("out_stored")
        dve_chain, topk_chain, sc_seen = sem("dve_chain"), sem("topk_chain"), sem("sc_seen")

        def w_count(n0, turn=0):
            return 16 * (n0 // 2 + 1) + turn * 16

        block = ctx.enter_context(nc.Block())

        @block.sync
        def _(sp):
            def load_w(n0, src, width=CH, turn=0):
                if n0 >= 2:
                    sp.wait_ge(lo_done, n0 - 1 + turn * 2)
                sp.dma_start(w_raw[n0 % 2][:, 0:width], src).then_inc(w_loaded[n0 % 2], 16)

            def load_ada(g0, slots, row, turn=0, per=0):
                if g0 >= slots:
                    sp.wait_ge(ada_used, g0 - slots + 1 + turn * per)
                s = g0 % slots
                sp.dma_start(ada_w[s][:], wada_d[row]).then_inc(ada_loaded[s], 16)

            sp.dma_start(X[:], x_d).then_inc(x_loaded, 16)
            for s in range(4):
                load_ada(s, 4, s)
            with sp.Fori(0, 7) as i:
                for s in range(4):
                    load_ada(4 + s, 4, 4 + s + i * 4, i, 4)
            load_w(0, win_d[0])
            load_w(1, win_d[1])
            for m in range(4):
                load_ada(32 + m, 2, 32 + m)
            with sp.Fori(0, NLAT // 2) as i:
                for u in range(2):
                    load_w(J_LAT + 1 + u, win_d[J_LAT + 1 + u + i * 2], turn=i)
                    for m in range(2):
                        load_ada(36 + 2 * u + m, 2, 36 + 2 * u + m + i * 4, i, 4)
            load_w(12, win_d[12])
            with sp.Fori(0, NC_T - 1) as i:
                for u in range(2):
                    load_w(13 + u, win_d[13 + u + i * 2], turn=i)
            load_w(J_QR, wqr_d[0], KQ * 2 * P)
            load_w(J_QR + 1, wqr_d[1], KQ * 2 * P)
            load_w(J_HEAD, whd_d[0], (KQ + 2 * KKV) * P)
            load_w(J_HEAD + 1, whd_d[1], (KQ + 2 * KKV) * P)
            for m in range(8):
                load_ada(56 + m, 2, 56 + m)
            for m in range(2):
                load_ada(64 + m, 2, 64 + m)
            with sp.Fori(0, 3) as i:
                for u in range(2):
                    load_w(J_HEAD + 2 + u, whd_d[2 + u + i * 2], (KQ + 2 * KKV) * P, turn=i)
                    for m in range(2):
                        load_ada(66 + 2 * u + m, 2, 66 + 2 * u + m + i * 4, i, 4)
            load_w(J_OUT, wout_d[0])
            for m in range(2):
                load_ada(78 + m, 2, 78 + m)
            with sp.Fori(0, 7) as i:
                for u in range(2):
                    load_w(J_OUT + 1 + u, wout_d[1 + u + i * 2], turn=i)
                    load_ada(80 + u, 2, 80 + u + i * 2, i, 2)
            load_w(J_OUT + 15, wout_d[15])
            load_ada(94, 2, 94)
            load_w(J_WQ, wwq_d[0])
            load_ada(95, 2, 95)
            for s in range(2):
                sp.wait_ge(bank_used[s], LEAD + BU_OUT_END[s])
            sp.dma_start(x1_d, X[:]).then_inc(x1_stored, 16)
            load_w(J_WQ + 1, wwq_d[1])
            with sp.Fori(0, 7) as i:
                for u in range(2):
                    load_w(J_WQ + 2 + u, wwq_d[2 + u + i * 2], turn=i)
            with sp.Fori(0, NKEY // 2) as i:
                for u in range(2):
                    load_w(J_U + u, u_d[u + i * 2], turn=i)
            load_w(J_V, v_d[0])
            load_w(J_V + 1, v_d[1])
            for s in range(2):
                sp.wait_ge(gelu_stored[s], DMA_LEAD + 16 * NKEY // 2)
                sp.wait_ge(g_stored[s], DMA_LEAD + 16 * 4)

            def load_weights_of(u, turn, q_pass):
                rows = bass.ds(turn * 4 + 2 * u, 2)
                sp.wait_ge(wt_ready[u], LEAD + turn + 32 * q_pass)
                sp.dma_start(gelu_l[u][:], gelu_d[rows].rearrange("e p t -> p e t")).then_inc(wt_loaded[u], 16)
                sp.dma_start(gate_l2[u][:], gate_d[:, :, rows, :].rearrange("c p i t -> p c i t")).then_inc(wt_loaded[u], 16)

            for q_pass in range(2):
                with sp.Fori(0, 32 - q_pass) as i:
                    for u in range(2):
                        load_weights_of(u, i, q_pass)
                        load_w(J_V + 64 * q_pass + 2 + u, v_d[64 * q_pass + 2 + u + i * 2], turn=i)
            for u in range(2):
                load_weights_of(u, 31, 1)

        @block.gpsimd
        def _(pool):
            def done(ins, n):
                ins.then_inc(pool_chain, 1)
                pool.wait_ge(pool_chain, n)

            done(pool.iota(iota_i[:], pattern=[[1, P]], base=0, channel_multiplier=0), 1)
            done(pool.iota(pidx_i[:], pattern=[[0, 1]], base=0, channel_multiplier=1), 2)
            done(pool.memset(ones[:], 1.0), 3)
            done(pool.memset(eps_c, EPS), 4)
            for s in range(2):
                done(pool.memset(half[s][64 * s:64 * s + 64, :], 1.0), 5 + 2 * s)
                done(pool.memset(half[s][64 - 64 * s:128 - 64 * s, :], 0.0), 6 + 2 * s)
            pool.sem_inc(const_ready, 1)

        @block.scalar
        def _(act):
            def hi(n0, turn=0):
                act.wait_ge(w_loaded[n0 % 2], w_count(n0, turn))
                if n0 >= 2:
                    act.wait_ge(pe_jobs, n0 - 1 + turn * 2)
                act.activation(w_hi[n0 % 2][:], w_raw[n0 % 2][:], ACT.Copy).then_inc(hi_done, 1)

            def squares(src, n, done0):
                for k in range(n):
                    if done0 + k >= 2:
                        act.wait_ge(sq_used, done0 + k - 1)
                    act.activation(sq[(done0 + k) % 2][:], src(k), ACT.Square).then_inc(sq_ready, 1)

            def modulate(which, ready):
                for k in range(KD):
                    act.wait_ge(scaled, which * KD + k + 1)
                    act.activation(X[:, k, :], X[:, k, :], ACT.Identity,
                                   bias=mod[:, (3 * which) * KD + k:(3 * which) * KD + k + 1]).then_inc(shifted_s, 1)
                    act.wait_ge(shifted_s, which * KD + k + 1)
                    act.activation(act_hi[:, k, :], X[:, k, :], ACT.Copy).then_inc(h_hi, 1)

            for q in (att_ready, sig_ready, exp_ready, qt_ready, *g_copied):
                act.sem_inc(q, LEAD)
            for q in (*gelu_stored, *g_stored):
                act.sem_inc(q, DMA_LEAD)
            act.dma_start(c_all[:], c_d.partition_broadcast(P)).then_inc(c_loaded, 16)
            act.dma_start(prm[:], prm_d).then_inc(small_loaded, 16)
            act.dma_start(pos_i[:], pos_d.partition_broadcast(P)).then_inc(small_loaded, 16)
            act.wait_ge(c_loaded, 16)
            act.activation(c_all[:], c_all[:], ACT.Silu).then_inc(c_ready, 1)
            act.wait_ge(angle_ready, 1)
            act.activation(sin_t[:], sin_t[:], ACT.Sin).then_inc(trig_ready, 1)
            act.activation(cos_t[:], cos_t[:], ACT.Sin).then_inc(trig_ready, 1)
            act.wait_ge(const_ready, 1)
            act.wait_ge(x_loaded, 16)
            squares(lambda k: X[:, k, :], KD, 0)
            act.wait_ge(sum_ready, 1)
            act.activation(root[:], bank[2][:], ACT.Sqrt, bias=eps_c, scale=1.0 / D).then_inc(root_ready, 1)
            modulate(0, None)
            hi(0)
            hi(1)

            def keep_latent(n0, turn=None):
                t = 0 if turn is None else turn
                act.wait_ge(pe_jobs, n0 + 1 + t * 2)
                act.activation(lat[:, n0 + t * 2, :] if turn is not None else lat[:, n0, :], bank[n0 % 2][:],
                               ACT.Copy).then_inc(bank_used[n0 % 2], 1)

            keep_latent(0)
            with act.Fori(0, NLAT // 2) as i:
                for u in range(2):
                    hi(J_LAT + 1 + u, i)
                    keep_latent(J_LAT + u, i)
            for s in range(2):
                act.wait_ge(bank_used[s], LEAD + BU_LAT_END[s])
            squares(lambda k: lat[:, 1 + k, :], NLAT, KD)
            act.activation(kr_sq[:], lat[:, 0, :], ACT.Square).then_inc(rope_sq, 1)
            act.wait_ge(sum_ready, 2)
            act.wait_ge(rstd_ready, 1)
            act.activation(root[:], bank[2][:], ACT.Sqrt, bias=eps_c, scale=1.0 / Q_LORA).then_inc(root_ready, 1)
            act.wait_ge(sum_ready, 3)
            act.wait_ge(rstd_ready, 2)
            act.activation(root[:], bank[3][:], ACT.Sqrt, bias=eps_c, scale=1.0 / KV_LORA).then_inc(root_ready, 1)

            def swap_halves(count):
                act.wait_ge(rope_g, count)
                for q in range(4):
                    src = tap_a[32 * (q ^ 1):32 * (q ^ 1) + 32, :]
                    act.activation(swapped[32 * q:32 * q + 32, :], src, ACT.Copy,
                                   scale=-1.0 if q % 2 == 0 else 1.0).then_inc(rope_sw, 1)

            swap_halves(1)
            hi(12)
            with act.Fori(0, NC_T) as i:
                hi(13, i)
                act.wait_ge(pe_jobs, 13 + i * 2)
                act.wait_ge(val_used, LEAD + i)
                act.activation(sig[:], bank[0][:], ACT.Sigmoid).then_inc(sig_ready, 1)
                hi(14, i)
            act.wait_ge(lat_scaled, NLAT)
            act.wait_ge(pe_jobs, J_QR)
            for k in range(NLAT):
                act.activation(act_hi[:, k, :], lat[:, 1 + k, :], ACT.Copy).then_inc(lat_hi, 1)
            for t in range(4):
                act.wait_ge(qr_ready, t + 1)
                act.activation(sq_qr[:, t, :], bank[[0, 1, 4, 5][t]][:], ACT.Square).then_inc(rope_sq, 1)
                swap_halves(2 + t)
                if t % 2 == 1:
                    hi(J_HEAD + t // 2)

            def project_post(u, i):
                n = J_HEAD + u
                act.wait_ge(q_ready, u + 1 + i * 2)
                act.wait_ge(ssq_ready, 2 * u + i * 4)
                act.activation(sq_q[:], bank[0][:], ACT.Square).then_inc(sqn_ready, 1)
                act.wait_ge(k_ready, u + 1 + i * 2)
                act.activation(sq_k[:], bank[1][:], ACT.Square).then_inc(sqn_ready, 1)
                for r in range(2):
                    act.wait_ge(ssq_ready, 2 * u + r + 1 + i * 4)
                    act.wait_ge(hrstd_ready, 2 * u + r + i * 4)
                    act.activation(root[:], bank[3][:], ACT.Sqrt, bias=eps_c,
                                   scale=1.0 / (NOPE + ROPE)).then_inc(hroot_ready, 1)
                act.wait_ge(pe_jobs, n + 1 + i * 2)
                act.activation(v_s[u][:], bank[2][:], ACT.Copy).then_inc(v_copied, 1)

            def attend(u, i):
                for qb in range(TB):
                    w = (qb + 1) * P
                    s = qb % 2
                    act.wait_ge(max_ready, 4 * u + qb + 1 + i * 8)
                    if qb >= 2:
                        act.wait_ge(tr_ready, LEAD + 4 * u + qb - 1 + i * 8)
                    else:
                        act.wait_ge(tr_ready, LEAD + 4 * u + i * 8)
                    act.activation(prob[s][:, 0:w], hb[s][:, 0:w], ACT.Exp, bias=nmx[s], scale=SCALE,
                                   accum_out=rsum[s]).then_inc(exp_ready, 1)
                act.wait_ge(pv_ready, LEAD + u + 1 + i * 2)
                act.activation(att_o[:, u + i * 2, :], bank[4][:], ACT.Copy).then_inc(att_ready, 1)

            project_post(0, 0)
            hi(J_HEAD + 2)
            with act.Fori(0, 3) as i:
                project_post(1, i)
                hi(J_HEAD + 3, i)
                attend(0, i)
                project_post(0, i + 1)
                hi(J_HEAD + 4, i)
                attend(1, i)
            project_post(1, 3)
            attend(0, 3)
            attend(1, 3)

            act.wait_ge(mean_sum, 1)
            act.activation(root[:], bank[2][:], ACT.Copy, scale=1.0 / CONV_CH).then_inc(mean_ready, 1)
            for k in range(NC_T):
                act.wait_ge(centred, k + 1)
                act.wait_ge(sq_used, KD + NLAT + k - 1)
                act.activation(sq[k % 2][:], conv_o[:, k, :], ACT.Square).then_inc(sq_ready, 1)
            for k in range(HEADS):
                if k >= 2:
                    act.wait_ge(mix_lo, k - 1)
                act.activation(act_hi[:, NC_T + k, :], att_o[:, k, :], ACT.Copy).then_inc(mix_hi, 1)
            act.wait_ge(var_sum, 1)
            act.activation(root[:], bank[3][:], ACT.Sqrt, bias=eps_c, scale=1.0 / CONV_CH).then_inc(root_ready, 1)
            for k in range(NC_T):
                act.wait_ge(ln_scaled, k + 1)
                act.activation(conv_o[:, k, :], conv_o[:, k, :], ACT.Silu, bias=pcol("ln_b", k),
                               scale=pcol("ln_g", k)).then_inc(ln_silu, 1)
                act.wait_ge(ln_silu, k + 1)
                act.activation(act_hi[:, k, :], conv_o[:, k, :], ACT.Copy).then_inc(mix_hi, 1)
            act.dma_start(keys[:], keys_d).then_inc(keys_loaded, 16)
            act.wait_ge(mix_lo, 2 * NC_T)
            act.dma_start(X[:], x_d).then_inc(x2_loaded, 16)
            hi(J_OUT + 1)
            with act.Fori(0, 7) as i:
                for u in range(2):
                    hi(J_OUT + 2 + u, i)
            hi(J_OUT + 16)

            for k in range(KD):
                act.wait_ge(bank_used[(J_OUT + k) % 2], LEAD + BU_OUT0[(J_OUT + k) % 2] + k // 2 + 1)
                act.wait_ge(sq_used, 34 + k - 1)
                act.activation(sq[k % 2][:], X[:, k, :], ACT.Square).then_inc(sq_ready, 1)
            act.wait_ge(sum_ready, 4)
            act.activation(root[:], bank[2][:], ACT.Sqrt, bias=eps_c, scale=1.0 / D).then_inc(root_ready, 1)
            modulate(1, None)
            hi(J_WQ + 1)

            with act.Fori(0, PH_) as i:
                act.wait_ge(pe_jobs, J_WQ + 1 + i * 2)
                act.wait_ge(sc_ready, LEAD + i * TB)
                act.activation(q_t[0][:], bank[J_WQ % 2][:], ACT.Copy).then_inc(qt_ready, 1)
                hi(J_WQ + 2, i)
                act.wait_ge(pe_jobs, J_WQ + 2 + i * 2)
                act.activation(q_t[1][:], bank[(J_WQ + 1) % 2][:], ACT.Copy).then_inc(qt_ready, 1)
                hi(J_WQ + 3, i)

            def gelu_job(u, turn):
                hi(J_U + 2 + u, turn)
                act.wait_ge(gelu_stored[u], DMA_LEAD + turn * 16)
                act.activation(gelu_s[u][:], bank[(J_U + u) % 2][:], ACT.Gelu_apprx_tanh).then_inc(bank_used[(J_U + u) % 2], 1)

            def gelu_store(u, turn):
                b = (J_U + u) % 2
                act.wait_ge(bank_used[b], LEAD + BU_U0[b] + 1 + turn)
                act.dma_start(gelu_d[turn * 2 + u], gelu_s[u][:]).then_inc(gelu_stored[u], 16)

            with act.Fori(0, TB) as i:
                act.wait_ge(gmax_ready, 1 + i)
                act.activation(expd[:], shifted[:], ACT.Exp).then_inc(gexp_ready, 1)
                for u in range(2):
                    gelu_job(u, i)
                    gelu_store(u, i)
            with act.Fori(4, 32) as i:
                for u in range(2):
                    gelu_job(u, i)
                    gelu_store(u, i)
            with act.Fori(0, 4) as c:
                for cb in range(2):
                    act.wait_ge(g_stored[cb], DMA_LEAD + c * 16)
                    with act.Fori(0, 4) as b:
                        turn = c * 8 + (4 * cb) + b
                        for u in range(2):
                            gelu_job(u, turn + 32)
                            gelu_store(u, turn + 32)
                            for g in range(2):
                                act.wait_ge(hot_used[2 * u + g], LEAD + turn + 1)
                                act.activation(g_chunk[cb][:, :, bass.ds(b * 16 + (8 * u + 4 * g), 4)],
                                               bank[2 + g][:].rearrange("p (t i) -> p i t", t=4),
                                               ACT.Copy).then_inc(g_copied[g], 1)
                    for g in range(2):
                        act.wait_ge(g_copied[g], LEAD + c * 16 + 8 * cb + 8)
                    act.dma_start(gate_d[c * 2 + cb], g_chunk[cb][:]).then_inc(g_stored[cb], 16)
            act.dma_start(x1_s[:], x1_d[:, 0:8, :]).then_inc(x1_loaded, 16) if False else None

            for s in range(2):
                act.wait_ge(g_stored[s], DMA_LEAD + 16 * 4)
                act.wait_ge(gelu_stored[s], DMA_LEAD + 16 * NKEY // 2)
            act.wait_ge(hot_used[3], LEAD + 32)
            act.dma_start(x1_s[:], x1_d[:, 0:8, :]).then_inc(x1_loaded, 16)

            def weigh_hi(u, turn):
                act.wait_ge(wt_ready[u], LEAD + turn + 1)
                act.activation(wt_hi[u][:], wt[u][:], ACT.Copy).then_inc(wth_ready[u], 1)

            weigh_hi(0, 0)
            weigh_hi(1, 0)
            for q_pass in range(2):
                with act.Fori(0, 32 - q_pass) as i:
                    for u in range(2):
                        hi(J_V + 64 * q_pass + 2 + u, i)
                        weigh_hi(u, i + 1 + 32 * q_pass)
                act.wait_ge(y_ready, 8 * q_pass + 8)
                act.dma_start(out_d[:, 8 * q_pass:8 * q_pass + 8, :], out_s[:]).then_inc(out_stored, 16)
                if q_pass == 0:
                    act.dma_start(x1_s[:], x1_d[:, 8:16, :]).then_inc(x1_loaded, 16)
            act.wait_ge(out_stored, 32)

        @block.vector
        def _(dve):
            T_ = Tally(dve, dve_chain)

            def lo(n0, turn=0):
                dve.wait_ge(hi_done, n0 + 1 + turn * 2)
                s = n0 % 2
                dve.tensor_tensor(w_lo[s][:], w_raw[s][:], w_hi[s][:].bitcast(F32), ALU.subtract).then_inc(lo_done, 1)

            def ada(g0, slots, count, col, turn=0):
                s = g0 % slots
                dve.wait_ge(ada_loaded[s], 16 * count + turn * 16)
                dve.scalar_tensor_tensor(out=ada_w[s][:], in0=ada_w[s][:], scalar=1.0, in1=c_all[:], op0=ALU.mult,
                                         op1=ALU.mult, accum_out=col).then_inc(ada_used, 1)

            def ada_mid(m0, turn=0, per=0):
                g0 = 32 + m0
                col = mod_raw[:, bass.ds(turn * per + g0, 1)] if per else mod_raw[:, g0:g0 + 1]
                s = g0 % 2
                dve.wait_ge(ada_loaded[s], 16 * (8 + m0 // 2 + 1) + (turn * (8 * per) if per else 0))
                dve.scalar_tensor_tensor(out=ada_w[s][:], in0=ada_w[s][:], scalar=1.0, in1=c_all[:], op0=ALU.mult,
                                         op1=ALU.mult, accum_out=col).then_inc(ada_used, 1)

            for q in (val_used, pt_ready, sc_used, *wt_ready):
                dve.sem_inc(q, LEAD)
            dve.wait_ge(const_ready, 1)
            T_.mark(dve.tensor_copy(iota_f[:], iota_i[:]))
            T_.step(dve.tensor_copy(pidx, pidx_i[:]))
            T_.step(dve.tensor_scalar(ident[:], iota_f[:], pidx, None, ALU.is_equal))

            dve.wait_ge(small_loaded, 32)
            PI = 3.1415925
            C1, C2 = 6.28125, 0.0019350051879882812
            C3 = 6.283185307179586 - C1 - C2
            MAGIC = 12582912.0
            T_.step(dve.tensor_copy(tap_a[:], pos_i[:])) if False else None
            ang, turns_ = root, rstd
            T_.step(dve.tensor_copy(ang[:], pos_i[:]))
            T_.step(dve.tensor_scalar(ang[:], ang[:], pcol("inv_freq"), None, ALU.mult))
            T_.step(dve.tensor_scalar(turns_[:], ang[:], 1.0 / 6.283185307179586, MAGIC, ALU.mult, ALU.add))
            T_.step(dve.tensor_scalar(turns_[:], turns_[:], -MAGIC, None, ALU.add))
            for cc in (C1, C2, C3):
                T_.step(dve.scalar_tensor_tensor(out=ang[:], in0=turns_[:], scalar=-cc, in1=ang[:], op0=ALU.mult, op1=ALU.add))
            T_.step(dve.tensor_scalar(cos_t[:], ang[:], 1.5707963267948966, None, ALU.add))
            T_.step(dve.tensor_scalar(turns_[:], cos_t[:], PI, -6.283185307179586, ALU.is_gt, ALU.mult))
            T_.step(dve.tensor_tensor(cos_t[:], cos_t[:], turns_[:], ALU.add))
            T_.step(dve.tensor_scalar(cos_t[:], cos_t[:], PI, -PI, ALU.min, ALU.max))
            dve.tensor_scalar(sin_t[:], ang[:], PI, -PI, ALU.min, ALU.max).then_inc(angle_ready, 1)
            dve.wait_ge(angle_ready, 1)

            dve.wait_ge(c_ready, 1)
            with dve.Fori(0, 8) as i:
                for s in range(4):
                    ada(s, 4, 1, mod_raw[:, bass.ds(i * 4 + s, 1)], i)
            dve.wait_ge(ada_used, 32)
            T_.step(dve.tensor_tensor(mod[:, 0:32], mod_raw[:, 0:32], pcol("b_ada", 0, 32), ALU.add))
            T_.step(dve.scalar_tensor_tensor(out=amp[:, 0, :], in0=mod[:, KD:2 * KD], scalar=1.0,
                                             in1=pcol("g1", 0, KD), op0=ALU.add, op1=ALU.mult))

            def modulate(which):
                def low(k):
                    dve.wait_ge(h_hi, which * KD + k + 1)
                    dve.tensor_tensor(act_lo[:, k, :], X[:, k, :], act_hi[:, k, :].bitcast(F32), ALU.subtract).then_inc(h_lo, 1)
                for k in range(KD):
                    dve.scalar_tensor_tensor(out=X[:, k, :], in0=X[:, k, :], scalar=amp[:, which, k:k + 1],
                                             in1=rstd[:], op0=ALU.mult, op1=ALU.mult).then_inc(scaled, 1)
                    if k >= 2:
                        low(k - 2)
                low(KD - 2)
                low(KD - 1)

            dve.wait_ge(root_ready, 1)
            dve.reciprocal(rstd[:], root[:]).then_inc(rstd_ready, 1)
            dve.wait_ge(rstd_ready, 1)
            modulate(0)
            lo(0)
            lo(1)
            for m in range(4):
                ada_mid(m)
            with dve.Fori(0, NLAT // 2) as i:
                for u in range(2):
                    lo(J_LAT + 1 + u, i)
                    for m in range(2):
                        ada_mid(4 + 2 * u + m, i, 4)
            for r, (a, n, g) in enumerate(((1, KQ, "qa_g"), (1 + KQ, KKV, "kva_g"))):
                dve.wait_ge(root_ready, 2 + r)
                if r:
                    dve.wait_ge(lat_scaled, KQ)
                dve.reciprocal(rstd[:], root[:]).then_inc(rstd_ready, 1)
                dve.wait_ge(rstd_ready, 2 + r)
                for k in range(n):
                    dve.scalar_tensor_tensor(out=lat[:, a + k, :], in0=lat[:, a + k, :], scalar=pcol(g, k),
                                             in1=rstd[:], op0=ALU.mult, op1=ALU.mult).then_inc(lat_scaled, 1)

            def rope(src, gain, out, count):
                dve.tensor_scalar(tap_a[:], src, gain, None, ALU.mult).then_inc(rope_g, 1)
                dve.wait_ge(rope_g, count)
                T_.mark(dve.tensor_tensor(tap_b[:], tap_a[:], cos_t[:], ALU.mult))
                dve.wait_ge(rope_sw, 4 * count)
                T_.step(dve.tensor_tensor(swapped[:], swapped[:], sin_t[:], ALU.mult))
                dve.tensor_tensor(out, tap_b[:], swapped[:], ALU.add).then_inc(rope_done, 1)
                dve.wait_ge(rope_done, count)

            dve.wait_ge(trig_ready, 2)
            rope(lat[:, 0, :], pcol("kr_g"), kr_rot[:], 1)
            lo(12)
            T_.step(dve.memset(glu[:, 0:CONV_W - 1], 0.0))
            with dve.Fori(0, NC_T) as i:
                T_.open(i, 4 + CONV_W)
                lo(13, i)
                k1 = T_.mark(dve.tensor_copy(conv_ws[:, 0:CONV_W], prm[:, bass.ds(i * CONV_W + COL["conv_w"][0], CONV_W)]))
                k2 = T_.mark(dve.tensor_copy(conv_ws[:, CONV_W:CONV_W + 1], prm[:, bass.ds(i + COL["conv_b"][0], 1)]))
                dve.wait_ge(sig_ready, LEAD + i + 1)
                dve.tensor_tensor(glu[:, CONV_W - 1:], bank[1][:], sig[:], ALU.mult).then_inc(val_used, 1)
                dve.wait_ge(val_used, LEAD + i + 1)
                T_.after(k2)
                acc, last = [tap_a, tap_b], [0, 0]
                for k in range(CONV_W):
                    w = conv_ws[:, k:k + 1]
                    src = glu[:, k:k + T]
                    a = k % 2
                    if k >= 2:
                        T_.after(last[a])
                    if k == 0:
                        ins = dve.tensor_scalar(tap_a[:], src, w, conv_ws[:, CONV_W:CONV_W + 1], ALU.mult, ALU.add)
                    elif k == 1:
                        ins = dve.tensor_scalar(tap_b[:], src, w, None, ALU.mult)
                    else:
                        ins = dve.scalar_tensor_tensor(out=acc[a][:], in0=src, scalar=w, in1=acc[a][:], op0=ALU.mult, op1=ALU.add)
                    last[a] = T_.mark(ins)
                    if k == CONV_W // 2:
                        lo(14, i)
                T_.after(max(last))
                T_.mark(dve.tensor_tensor(conv_o[:, i, :], tap_a[:], tap_b[:], ALU.add))
                T_.step(dve.tensor_copy(conv_ws[:, 0:1], conv_ws[:, 0:1]))
                T_.close(NC_T)
            dve.tensor_copy(tiny[:, 10:11], tiny[:, 0:1]).then_inc(conv_done, 1)

            for k in range(NLAT):
                dve.wait_ge(lat_hi, k + 1)
                dve.tensor_tensor(act_lo[:, 6 + k, :], lat[:, 1 + k, :], act_hi[:, k, :].bitcast(F32), ALU.subtract).then_inc(lat_lo, 1)
            for t in range(4):
                dve.wait_ge(rope_sq, 2 + t)
                rope(bank[[0, 1, 4, 5][t]][:], pcol("qr_g"), qr_rot[:, t, :], 2 + t)
                if t % 2 == 1:
                    lo(J_HEAD + t // 2)
            for m in range(8):
                ada_mid(24 + m)

            def project_post(u, i):
                r0, r1 = 64 * u, 64 * u + 64
                dve.wait_ge(hroot_ready, 2 * u + 1 + i * 4)
                dve.wait_ge(qk_ready, u + i * 2)
                dve.reciprocal(rstd[:], root[:]).then_inc(hrstd_ready, 1)
                dve.wait_ge(hrstd_ready, 2 * u + 1 + i * 4)
                dve.scalar_tensor_tensor(out=q_n[u][:], in0=bank[0][:], scalar=pcol("qn_g"), in1=rstd[:],
                                         op0=ALU.mult, op1=ALU.mult).then_inc(q_used, 1)
                T_.step(dve.tensor_tensor(q_r[u][r0:r1, :], qr_rot[r0:r1, i, :], rstd[r0:r1, :], ALU.mult))
                dve.wait_ge(q_used, u + 1 + i * 2)
                dve.wait_ge(hroot_ready, 2 * u + 2 + i * 4)
                dve.reciprocal(rstd[:], root[:]).then_inc(hrstd_ready, 1)
                dve.wait_ge(hrstd_ready, 2 * u + 2 + i * 4)
                dve.scalar_tensor_tensor(out=k_n[u][:], in0=bank[1][:], scalar=pcol("kn_g"), in1=rstd[:],
                                         op0=ALU.mult, op1=ALU.mult).then_inc(k_used, 1)
                dve.tensor_tensor(k_r[u][r0:r1, :], kr_rot[r0:r1, :], rstd[r0:r1, :], ALU.mult).then_inc(qk_ready, 1)

            def attend(u, i):
                def row_max(qb):
                    w, s = (qb + 1) * P, qb % 2
                    dve.wait_ge(score_ready, 4 * u + qb + 1 + i * 8)
                    T_.step(dve.memset(hb[s][0:64, w - 64:w], NEG))
                    T_.step(dve.reduce_max(mx[s], hb[s][:, 0:w], AX_X))
                    dve.tensor_scalar(nmx[s], mx[s], -SCALE, None, ALU.mult).then_inc(max_ready, 1)

                def normalise(qb):
                    w, s = (qb + 1) * P, qb % 2
                    dve.wait_ge(exp_ready, LEAD + 4 * u + qb + 1 + i * 8)
                    T_.step(dve.reciprocal(rrec[s], rsum[s]))
                    dve.tensor_scalar(prob[s][:, 0:w], prob[s][:, 0:w], rrec[s], None, ALU.mult).then_inc(prob_ready, 1)

                def keep_t(qb):
                    w = (qb + 1) * P
                    if qb == 0:
                        dve.wait_ge(pv_ready, LEAD + u + i * 2)
                    dve.wait_ge(tr_ready, LEAD + 4 * u + qb + 1 + i * 8)
                    dve.tensor_copy(prob_t[:, 0:qb + 1, qb * P:qb * P + P],
                                    bank[7][:, 0:w].rearrange("p (j q) -> p j q", q=P)).then_inc(pt_ready, 1)

                row_max(0)
                row_max(1)
                normalise(0)
                row_max(2)
                keep_t(0)
                normalise(1)
                row_max(3)
                keep_t(1)
                normalise(2)
                keep_t(2)
                normalise(3)
                keep_t(3)

            PP, AT = 1, 12
            project_post(0, 0)
            lo(J_HEAD + 2)
            for m in range(2):
                ada_mid(32 + m)
            with dve.Fori(0, 3) as i:
                T_.open(i, 2 * PP + 2 * AT)
                for u in range(2):
                    project_post(1 - u, i + u)
                    lo(J_HEAD + 3 + u, i)
                    attend(u, i)
                    for m in range(2):
                        ada_mid(34 + 2 * u + m, i, 4)
                T_.close(3)
            project_post(1, 3)
            attend(0, 3)
            attend(1, 3)
            for m in range(2):
                ada_mid(46 + m)
            dve.wait_ge(ada_used, 80)
            T_.step(dve.tensor_tensor(mod[:, 32:80], mod_raw[:, 32:80], pcol("b_ada", 32, 48), ALU.add))
            T_.step(dve.scalar_tensor_tensor(out=amp[:, 1, :], in0=mod[:, 4 * KD:5 * KD], scalar=1.0,
                                             in1=pcol("g2", 0, KD), op0=ALU.add, op1=ALU.mult))

            dve.wait_ge(mean_ready, 1)
            for k in range(NC_T):
                dve.tensor_tensor(conv_o[:, k, :], conv_o[:, k, :], root[:], ALU.subtract).then_inc(centred, 1)
            for k in range(HEADS):
                dve.wait_ge(mix_hi, k + 1)
                dve.tensor_tensor(act_lo[:, NC_T + k, :], att_o[:, k, :], act_hi[:, NC_T + k, :].bitcast(F32),
                                  ALU.subtract).then_inc(mix_lo, 1)
            dve.wait_ge(root_ready, 4)
            dve.reciprocal(rstd[:], root[:]).then_inc(rstd_ready, 1)
            dve.wait_ge(rstd_ready, 4)
            dve.wait_ge(centred, NC_T)

            def conv_low(k):
                dve.wait_ge(mix_hi, HEADS + k + 1)
                dve.tensor_tensor(act_lo[:, k, :], conv_o[:, k, :], act_hi[:, k, :].bitcast(F32), ALU.subtract).then_inc(mix_lo, 1)
            for k in range(NC_T):
                dve.tensor_tensor(conv_o[:, k, :], conv_o[:, k, :], rstd[:], ALU.mult).then_inc(ln_scaled, 1)
                if k >= 2:
                    conv_low(k - 2)
            conv_low(NC_T - 2)
            conv_low(NC_T - 1)

            def residual(m, n0, turn=None):
                b = n0 % 2
                t = 0 if turn is None else turn
                dve.wait_ge(pe_jobs, n0 + 1 + t * 2)
                col = mod[:, bass.ds(t * 2 + 2 * KD + m, 1)] if turn is not None else mod[:, 2 * KD + m:2 * KD + m + 1]
                xt = X[:, m + t * 2, :] if turn is not None else X[:, m, :]
                dve.scalar_tensor_tensor(out=xt, in0=bank[b][:], scalar=col, in1=xt, op0=ALU.mult,
                                         op1=ALU.add).then_inc(bank_used[b], 1)

            lo(J_OUT + 1)
            dve.wait_ge(x2_loaded, 16)
            with dve.Fori(0, 7) as i:
                for u in range(2):
                    lo(J_OUT + 2 + u, i)
                    residual(u, J_OUT + u, i)
                    ada_mid(48 + u, i, 2)
            lo(J_OUT + 16)
            residual(14, J_OUT + 14)
            ada_mid(62)
            residual(15, J_OUT + 15)
            ada_mid(63)
            dve.wait_ge(ada_used, 96)
            T_.step(dve.tensor_tensor(mod[:, 80:96], mod_raw[:, 80:96], pcol("b_ada", 80, 16), ALU.add))

            dve.wait_ge(root_ready, 5)
            dve.reciprocal(rstd[:], root[:]).then_inc(rstd_ready, 1)
            dve.wait_ge(rstd_ready, 5)
            dve.wait_ge(x1_stored, 16)
            modulate(1)
            lo(J_WQ + 1)

            K_ = Tally(dve, topk_chain)

            def top16(jobs):
                a = [K_.mark(dve.max(v[:, 0:8], s)) for v, ix, s, left in jobs]
                b = []
                for (v, ix, s, left), k in zip(jobs, a):
                    K_.after(k)
                    b.append(K_.mark(dve.match_replace(left, v[:, 0:8], s, NEG)))
                c_ = [K_.mark(dve.max_index(ix[:, 0:8], v[:, 0:8], s)) for v, ix, s, left in jobs]
                d_ = []
                for (v, ix, s, left), k in zip(jobs, b):
                    K_.after(k)
                    d_.append(K_.mark(dve.max(v[:, 8:16], left)))
                for (v, ix, s, left), k in zip(jobs, d_):
                    K_.after(k)
                    e_ = K_.mark(dve.max_index(ix[:, 8:16], v[:, 8:16], left))
                return e_

            def select(b, h):
                S = bank[2 + b]
                dve.wait_ge(sc_ready, LEAD + b + 1 + h * TB)
                dve.sem_inc(sc_seen, 1)
                v1, v2 = val[0][:, b, :], val[1][:, b, :]
                K_.after(top16([(v1, idx[0][:, b, :], S[:, 0:NKEY], s_left[0][:]),
                                (v2, idx[1][:, b, :], S[:, NKEY:2 * NKEY], s_left[1][:])]))
                dve.sem_inc(sc_used, 1)
                K_.step(dve.tensor_tensor(cand[:].rearrange("p (a b) -> p a b", b=TOPK), v1.unsqueeze(2).broadcast_to([P, TOPK, TOPK]),
                                  v2.unsqueeze(1).broadcast_to([P, TOPK, TOPK]), ALU.add))
                return top16([(best[:, b, :], flat[:, b, :], cand[:], c_left[:])])

            with dve.Fori(0, PH_) as h:
                dve.sem_clear(topk_chain)
                K_.k = 0
                lo(J_WQ + 2, h)
                select(0, h)
                select(1, h)
                lo(J_WQ + 3, h)
                select(2, h)
                K_.after(select(3, h))
                K_.mark(dve.tensor_copy(flat_all[:, :, h, :], flat[:]))
                K_.mark(dve.tensor_copy(i1_all[:, :, h, :], idx[0][:]))
                K_.mark(dve.tensor_copy(i2_all[:, :, h, :], idx[1][:]))
                K_.step(dve.tensor_copy(best_all[:, :, h, :], best[:]))

            hot16 = iota_f[:, 0:TOPK].unsqueeze(1).broadcast_to([P, P, TOPK])

            with dve.Fori(0, TB) as b:
                T_.open(b, 12)
                fl = flat_all[:, b, :, :].rearrange("p h k -> p (h k)")
                bs = best_all[:, b, :, :]
                dve.tensor_tensor(shifted[:], bs, bs[:, :, 0:1].broadcast_to([P, PH_, TOPK]), ALU.subtract).then_inc(gmax_ready, 1)
                for half_i, (tab, ia, op, arg) in enumerate(((e1_t, i1_all, ALU.logical_shift_right, 4), (e2_t, i2_all, ALU.bitwise_and, 15))):
                    lo(J_U + 2 + half_i, b)
                    T_.step(dve.tensor_scalar(part[:], fl, arg, None, op))
                    T_.step(dve.tensor_tensor(pick[:].rearrange("p h k a -> p (h k) a"),
                                              part[:].unsqueeze(2).broadcast_to([P, P, TOPK]), hot16, ALU.is_equal))
                    T_.step(dve.tensor_tensor(pick[:], pick[:], ia[:, b, :, :].unsqueeze(2).broadcast_to([P, PH_, TOPK, TOPK]), ALU.mult))
                    T_.step(dve.tensor_reduce(tab[:, b, :], pick[:].rearrange("p h k a -> p (h k) a"), AX_X, ALU.add))
                dve.wait_ge(gexp_ready, 1 + b)
                T_.step(dve.reduce_sum(esum[:], expd[:], AX_X))
                T_.step(dve.reciprocal(ersum[:], esum[:]))
                T_.step(dve.tensor_tensor(gate_t[:, b, :].rearrange("p (h k) -> p h k", h=PH_), expd[:],
                                          ersum[:].unsqueeze(2).broadcast_to([P, PH_, TOPK]), ALU.mult))
                T_.mark(dve.tensor_copy(tiny[:, 11:12], tiny[:, 0:1]))
                T_.close(TB)
            dve.tensor_copy(tiny[:, 12:13], tiny[:, 0:1]).then_inc(tables_ready, 1)
            dve.wait_ge(tabt_ready, 3)
            T_.mark(dve.tensor_copy(e1_c[:], bank[2][:]))
            T_.mark(dve.tensor_copy(e2_c[:], bank[3][:]))
            T_.step(dve.tensor_copy(gate_h[:], bank[4][:]))
            T_.step(dve.tensor_tensor(gate_l[:], bank[4][:], gate_h[:].bitcast(F32), ALU.subtract))
            dve.tensor_copy(tiny[:, 12:13], tiny[:, 0:1]).then_inc(tabt_used, 1)

            with dve.Fori(4, 32) as i:
                for u in range(2):
                    lo(J_U + 2 + u, i)

            with dve.Fori(0, 32) as i:
                for u in range(2):
                    lo(J_U + 64 + 2 + u, i)
                    for g in range(2):
                        dve.wait_ge(hot_used[2 * u + g], LEAD + i)
                        for q in range(4):
                            s = 8 * u + 4 * g + q
                            tok = bass.ds(i * 16 + s, 1)
                            dve.tensor_scalar(hot2[:, s, :], iota_f[:], e2_c[:, tok], None, ALU.is_equal)
                            dve.tensor_scalar(hot1h[:, s, :], iota_f[:], e1_c[:, tok], gate_h[:, tok].bitcast(F32), ALU.is_equal, ALU.mult)
                            ins = dve.tensor_scalar(hot1l[:, s, :], iota_f[:], e1_c[:, tok], gate_l[:, tok], ALU.is_equal, ALU.mult)
                        ins.then_inc(hot_ready[2 * u + g], 1)

            def weigh(u, turn):
                dve.wait_ge(wt_loaded[u], (turn + 1) * 32)
                dve.tensor_tensor(wt[u][:].rearrange("p i (c t) -> p i c t", c=8), gelu_l[u][:].rearrange("p i (c t) -> p i c t", c=8),
                                  gate_l2[u][:].rearrange("p c i t -> p i c t"), ALU.mult).then_inc(wt_ready[u], 1)

            def weigh_lo(u, turn):
                dve.wait_ge(wth_ready[u], turn + 1)
                dve.tensor_tensor(wt_lo[u][:], wt[u][:], wt_hi[u][:].bitcast(F32), ALU.subtract).then_inc(wtl_ready[u], 1)

            for u in range(2):
                weigh(u, 0)
                weigh_lo(u, 0)
            for q_pass in range(2):
                with dve.Fori(0, 32 - q_pass) as i:
                    for u in range(2):
                        lo(J_V + 64 * q_pass + 2 + u, i)
                        weigh(u, i + 1 + 32 * q_pass)
                        weigh_lo(u, i + 1 + 32 * q_pass)
                dve.wait_ge(x1_loaded, 16 * (q_pass + 1))
                dve.wait_ge(pe_jobs, J_V + 64 * (q_pass + 1))
                if q_pass:
                    dve.wait_ge(out_stored, 16)
                for d in range(8):
                    m = 5 * KD + 8 * q_pass + d
                    dve.scalar_tensor_tensor(out=out_s[:, d, :], in0=bank[d][:], scalar=mod[:, m:m + 1], in1=x1_s[:, d, :],
                                             op0=ALU.mult, op1=ALU.add).then_inc(y_ready, 1)

        @block.tensor
        def _(pe):
            def dense(slot, out, nk, koff, hi_t, lo_t, before=None):
                for k in range(nk):
                    if before:
                        before(k)
                    wh = w_hi[slot][:, koff + k * P:koff + (k + 1) * P]
                    wl = w_lo[slot][:, koff + k * P:koff + (k + 1) * P]
                    pe.matmul(out, wh, hi_t(k), start=(k == 0), stop=False)
                    pe.matmul(out, wh, lo_t(k), start=False, stop=False)
                    last = pe.matmul(out, wl, hi_t(k), start=False, stop=(k == nk - 1))
                return last

            H = lambda k: act_hi[:, k, :]
            L = lambda k: act_lo[:, k, :]

            def job(n0, turn=0, used=None, before=None, hi_t=H, lo_t=L):
                pe.wait_ge(lo_done, n0 + 1 + turn * 2)
                if used is not None:
                    pe.wait_ge(*used)
                dense(n0 % 2, bank[n0 % 2][:], KD, 0, hi_t, lo_t, before).then_inc(pe_jobs, 1)

            def sums(n, out, done0):
                for k in range(n):
                    pe.wait_ge(sq_ready, done0 + k + 1)
                    last = pe.matmul(out[:], ones[:], sq[(done0 + k) % 2][:], start=(k == 0), stop=(k == n - 1))
                    if k < n - 1:
                        last.then_inc(sq_used, 1)
                last.then_inc(sq_used, 1)
                pe.wait_ge(sq_used, done0 + n)
                pe.sem_inc(sum_ready, 1)

            for q in (tr_ready, pv_ready, sc_ready, *hot_used, *bank_used):
                pe.sem_inc(q, LEAD)
            pe.wait_ge(const_ready, 1)
            sums(KD, bank[2], 0)
            job(0, before=lambda k: pe.wait_ge(h_lo, k + 1))
            with pe.Fori(0, NLAT // 2) as i:
                job(1, i, (bank_used[1], LEAD + i))
                job(2, i, (bank_used[0], LEAD + i + 1))
            sums(KQ, bank[2], KD)
            sums(KKV, bank[3], KD + KQ)
            for s in range(2):
                pe.wait_ge(bank_used[s], LEAD + BU_LAT_END[s])
            with pe.Fori(0, NC_T) as i:
                job(J_CONV, i, (val_used, LEAD + i))
                job(J_CONV + 1, i, (sig_ready, LEAD + i))
            pe.wait_ge(val_used, LEAD + NC_T)
            pe.wait_ge(sig_ready, LEAD + NC_T)
            LL = lambda k: act_lo[:, 6 + k, :]
            for j in range(2):
                pe.wait_ge(lo_done, J_QR + j + 1)
                for t in range(2):
                    last = dense((J_QR + j) % 2, bank[[0, 1, 4, 5][2 * j + t]][:], KQ, t * KQ * P, H, LL,
                                 (lambda k: pe.wait_ge(lat_lo, k + 1)) if j + t == 0 else None)
                    last.then_inc(qr_ready, 1)
                pe.wait_ge(qr_ready, 2 * j + 2)
                pe.sem_inc(pe_jobs, 1)
            pe.wait_ge(lat_lo, NLAT)
            pe.wait_ge(rope_sq, 5)
            pe.wait_ge(rope_done, 5)

            def project(u, i):
                s = (J_HEAD + u) % 2
                pe.wait_ge(lo_done, J_HEAD + u + 1 + i * 2)
                pe.wait_ge(q_used, u + i * 2)
                dense(s, bank[0][:], KQ, 0, H, LL).then_inc(q_ready, 1)
                pe.wait_ge(k_used, u + i * 2)
                Hk = lambda k: act_hi[:, KQ + k, :]
                Lk = lambda k: act_lo[:, 6 + KQ + k, :]
                dense(s, bank[1][:], KKV, KQ * P, Hk, Lk).then_inc(k_ready, 1)
                pe.wait_ge(v_copied, u + i * 2)
                for tb in range(TB):
                    tk = slice(tb * P, tb * P + P)
                    for k in range(KKV):
                        wv = slice((KQ + KKV + k) * P, (KQ + KKV + k + 1) * P)
                        o = bank[2][:, tk]
                        pe.matmul(o, Hk(k)[:, tk], w_hi[s][:, wv], start=(k == 0), stop=False)
                        pe.matmul(o, Lk(k)[:, tk], w_hi[s][:, wv], start=False, stop=False)
                        last = pe.matmul(o, Hk(k)[:, tk], w_lo[s][:, wv], start=False, stop=(k == KKV - 1))
                last.then_inc(pe_jobs, 1)
                pe.wait_ge(sqn_ready, 2 * u + 1 + i * 4)
                pe.wait_ge(hroot_ready, 2 * u + i * 4)
                pe.matmul(bank[3][:], ones[:], sq_q[:], start=True, stop=False)
                pe.matmul(bank[3][:], half[u][:], sq_qr[:, i, :], start=False, stop=True).then_inc(ssq_ready, 1)
                pe.wait_ge(sqn_ready, 2 * u + 2 + i * 4)
                pe.wait_ge(hroot_ready, 2 * u + 1 + i * 4)
                pe.matmul(bank[3][:], ones[:], sq_k[:], start=True, stop=False)
                pe.matmul(bank[3][:], half[0][:], kr_sq[:], start=False, stop=True).then_inc(ssq_ready, 1)

            def attend(u, i):
                r0, r1 = 64 * u, 64 * u + 64

                def score(qb):
                    w, qs = (qb + 1) * P, slice(qb * P, qb * P + P)
                    if qb == 0:
                        pe.wait_ge(qk_ready, u + 1 + i * 2)
                    if qb >= 2:
                        pe.wait_ge(exp_ready, LEAD + 4 * u + qb - 1 + i * 8)
                    elif qb == 0:
                        pe.wait_ge(exp_ready, LEAD + 4 * u + i * 8)
                    o = hb[qb % 2][:, 0:w]
                    pe.matmul(o, q_n[u][:, qs], k_n[u][:, 0:w], start=True, stop=False)
                    pe.matmul(o, q_r[u][r0:r1, qs], k_r[u][r0:r1, 0:w], start=False, stop=True).then_inc(score_ready, 1)

                def turn_probs(qb):
                    pe.wait_ge(prob_ready, 4 * u + qb + 1 + i * 8)
                    pe.wait_ge(pt_ready, LEAD + 4 * u + qb + i * 8)
                    for j in range(qb + 1):
                        last = pe.transpose(bank[7][:, j * P:(j + 1) * P], prob[qb % 2][:, j * P:(j + 1) * P], ident[:])
                    last.then_inc(tr_ready, 1)

                score(0)
                score(1)
                turn_probs(0)
                score(2)
                turn_probs(1)
                score(3)
                turn_probs(2)
                turn_probs(3)
                pe.wait_ge(pt_ready, LEAD + 4 * u + 4 + i * 8)
                pe.wait_ge(v_copied, u + 1 + i * 2)
                pe.wait_ge(att_ready, LEAD + u + i * 2)
                for j in range(TB):
                    last = pe.matmul(bank[4][:, j * P:], v_s[u][:, j * P:(j + 1) * P], prob_t[:, j, j * P:],
                                     start=(j == 0), stop=(j == TB - 1))
                last.then_inc(pv_ready, 1)

            project(0, 0)
            with pe.Fori(0, 3) as i:
                project(1, i)
                attend(0, i)
                project(0, i + 1)
                attend(1, i)
            project(1, 3)
            attend(0, 3)
            attend(1, 3)

            pe.wait_ge(conv_done, 1)
            for k in range(NC_T):
                last = pe.matmul(bank[2][:], ones[:], conv_o[:, k, :], start=(k == 0), stop=(k == NC_T - 1))
            last.then_inc(mean_sum, 1)
            for k in range(NC_T):
                pe.wait_ge(sq_ready, KD + NLAT + k + 1)
                last = pe.matmul(bank[3][:], ones[:], sq[k % 2][:], start=(k == 0), stop=(k == NC_T - 1))
                last.then_inc(sq_used, 1)
            pe.wait_ge(sq_used, KD + NLAT + NC_T)
            pe.sem_inc(var_sum, 1)

            order = list(range(NC_T, KD)) + list(range(NC_T))

            def out_job(n0, turn=0, used=None, first=False):
                s = n0 % 2
                pe.wait_ge(lo_done, n0 + 1 + turn * 2)
                if used:
                    pe.wait_ge(*used)
                for at_, k in enumerate(order):
                    if first:
                        pe.wait_ge(mix_lo, at_ + 1)
                    wh, wl = w_hi[s][:, k * P:(k + 1) * P], w_lo[s][:, k * P:(k + 1) * P]
                    pe.matmul(bank[s][:], wh, act_hi[:, k, :], start=(at_ == 0), stop=False)
                    pe.matmul(bank[s][:], wh, act_lo[:, k, :], start=False, stop=False)
                    last = pe.matmul(bank[s][:], wl, act_hi[:, k, :], start=False, stop=(at_ == KD - 1))
                last.then_inc(pe_jobs, 1)

            out_job(J_OUT, first=True)
            out_job(J_OUT + 1)
            with pe.Fori(0, 7) as i:
                for u in range(2):
                    b = (J_OUT + u) % 2
                    out_job(J_OUT + 2 + u, i, (bank_used[b], LEAD + i + BU_OUT0[b] + 1))
            for s in range(2):
                pe.wait_ge(bank_used[s], LEAD + BU_OUT_END[s])
            for k in range(KD):
                pe.wait_ge(sq_ready, 34 + k + 1)
                last = pe.matmul(bank[2][:], ones[:], sq[k % 2][:], start=(k == 0), stop=(k == KD - 1))
                last.then_inc(sq_used, 1)
            pe.wait_ge(sq_used, 34 + KD)
            pe.sem_inc(sum_ready, 1)

            pe.wait_ge(h_lo, 2 * KD)
            pe.wait_ge(keys_loaded, 16)
            with pe.Fori(0, PH_) as h:
                job(J_WQ, h, (qt_ready, LEAD + h * 2))
                job(J_WQ + 1, h, (qt_ready, LEAD + h * 2))
                pe.wait_ge(qt_ready, LEAD + 2 + h * 2)
                for b in range(TB):
                    ts_ = slice(b * P, b * P + P)
                    pe.wait_ge(sc_used, LEAD + b + h * TB)
                    for half_i in range(2):
                        last = pe.matmul(bank[2 + b][:, half_i * NKEY:(half_i + 1) * NKEY], q_t[half_i][:, ts_],
                                         keys[:, h, half_i, :], start=True, stop=True)
                    last.then_inc(sc_ready, 1)

            pe.wait_ge(qt_ready, LEAD + 2 * PH_)

            def u_job(u, turn):
                b = (J_U + u) % 2
                job(J_U + u, turn, (bank_used[b], LEAD + turn + BU_U0[b]))

            with pe.Fori(0, TB) as i:
                for u in range(2):
                    u_job(u, i)
            pe.wait_ge(tables_ready, 1)
            for t_i, tab in enumerate((e1_t, e2_t, gate_t)):
                for b in range(TB):
                    last = pe.transpose(bank[2 + t_i][:, b * P:(b + 1) * P], tab[:, b, :], ident[:])
                last.then_inc(tabt_ready, 1)
            with pe.Fori(4, 32) as i:
                for u in range(2):
                    u_job(u, i)
            pe.wait_ge(tabt_used, 1)
            with pe.Fori(0, 32) as i:
                for u in range(2):
                    u_job(u, i + 32)
                    for g in range(2):
                        pe.wait_ge(hot_ready[2 * u + g], i + 1)
                        pe.wait_ge(g_copied[g], LEAD + i * 2 + u)
                        for q in range(4):
                            s = 8 * u + 4 * g + q
                            o = bank[2 + g][:, q * P:(q + 1) * P]
                            pe.matmul(o, hot2[:, s, :], hot1h[:, s, :], start=True, stop=False)
                            last = pe.matmul(o, hot2[:, s, :], hot1l[:, s, :], start=False, stop=True)
                        last.then_inc(hot_used[2 * u + g], 1)

            for s in range(2):
                pe.wait_ge(bank_used[s], LEAD + BU_U_END[s])
                pe.wait_ge(g_copied[s], LEAD + 64)

            def v_job(q_pass, u, turn, start=False, stop=False):
                n0 = J_V + 64 * q_pass + u
                s = n0 % 2
                pe.wait_ge(lo_done, n0 + 1 + turn * 2)
                pe.wait_ge(wtl_ready[u], turn + 1 + 32 * q_pass)
                for e in range(2):
                    for d in range(8):
                        if start and e == 0 and q_pass:
                            pe.wait_ge(y_ready, d + 1)
                        col = slice(e * 1024 + d * P, e * 1024 + (d + 1) * P)
                        pe.matmul(bank[d][:], w_hi[s][:, col], wt_hi[u][:, e, :], start=(start and e == 0), stop=False)
                        pe.matmul(bank[d][:], w_hi[s][:, col], wt_lo[u][:, e, :], start=False, stop=False)
                        last = pe.matmul(bank[d][:], w_lo[s][:, col], wt_hi[u][:, e, :], start=False, stop=(stop and e == 1))
                last.then_inc(pe_jobs, 1)

            for q_pass in range(2):
                v_job(q_pass, 0, 0, start=True)
                v_job(q_pass, 1, 0)
                with pe.Fori(1, 31) as i:
                    for u in range(2):
                        v_job(q_pass, u, i)
                v_job(q_pass, 0, 31)
                v_job(q_pass, 1, 31, stop=True)


BU_LAT_END = [6, 5]
BU_OUT0 = [6, 5]
BU_OUT_END = [BU_OUT0[0] + 8, BU_OUT0[1] + 8]
BU_U0 = BU_OUT_END
BU_U_END = [BU_U0[0] + 64, BU_U0[1] + 64]


def kernel(**inputs):
    import numpy as np
    import concourse.bacc as bacc
    from concourse.bass_utils import run_bass_kernel_spmd

    a = {k: np.asarray(v) for k, v in inputs.items()}

    def tiles(w, n_out):
        k = w.shape[0] // P
        return w.reshape(k, P, n_out, P).transpose(2, 1, 0, 3).reshape(n_out, P, k * P)

    def cols(v):
        return v.reshape(-1, P).T

    w_in = a["w_in"][0]
    o1 = 2 * CONV_CH
    conv_pairs = np.stack([w_in[:, :CONV_CH].reshape(D, NC_T, P), w_in[:, CONV_CH:o1].reshape(D, NC_T, P)], 2).reshape(D, o1)
    kr = w_in[:, o1 + Q_LORA + KV_LORA:]
    win = tiles(np.concatenate([kr, kr, w_in[:, o1:o1 + Q_LORA + KV_LORA], conv_pairs], 1), 1 + NLAT + 2 * NC_T)
    uq = a["w_uq"][0].reshape(Q_LORA, HEADS, NOPE + ROPE)
    ukv = a["w_ukv"][0].reshape(KV_LORA, HEADS, NOPE + VH)
    qr = tiles(uq[:, :, NOPE:].reshape(Q_LORA, 4 * P), 4).reshape(2, 2, P, KQ * P).transpose(0, 2, 1, 3).reshape(2, P, 2 * KQ * P)
    hd = np.concatenate([tiles(uq[:, :, :NOPE].reshape(Q_LORA, -1), HEADS), tiles(ukv[:, :, :NOPE].reshape(KV_LORA, -1), HEADS),
                         tiles(ukv[:, :, NOPE:].reshape(KV_LORA, -1), HEADS)], 2)
    keys = np.stack([a["peer_k1"][0], a["peer_k2"][0]], 1).transpose(3, 0, 1, 2)
    u_t = a["peer_u"][0].reshape(NKEY, P, KD, P).transpose(0, 3, 2, 1).reshape(NKEY, P, CH)
    v_t = a["peer_v"][0].reshape(64, 2, P, 2, 1024).transpose(3, 0, 2, 1, 4).reshape(NKEY, P, CH)
    wada = a["w_ada"][0].T.reshape(6 * KD, P, D)
    conv_w = a["conv_dw_w"][0].reshape(CONV_W, NC_T, P).transpose(2, 1, 0).reshape(P, NC_T * CONV_W)
    inv = (10000.0 ** (-np.arange(0, ROPE, 2, dtype=np.float32) / ROPE)).astype(np.float32)
    qg, kg = a["q_norm_g"][0], a["k_norm_g"][0]
    two = lambda v: np.concatenate([v, v])[:, None]
    prm = np.concatenate([cols(a["norm1_g"][0]), cols(a["norm2_g"][0]), cols(a["conv_dw_b"][0]), cols(a["conv_ln_g"][0]),
                          cols(a["conv_ln_b"][0]), conv_w, cols(a["q_a_norm_g"][0]), cols(a["kv_a_norm_g"][0]),
                          qg[:NOPE, None], two(qg[NOPE:]), kg[:NOPE, None], two(kg[NOPE:]), cols(a["b_ada"][0]),
                          np.tile(inv, 4)[:, None]], 1)
    x_t = a["x"][0].T.reshape(KD, P, T).transpose(1, 0, 2)
    arrays = dict(x=x_t, c=a["c"].reshape(D), pos=a["positions"].reshape(T), prm=prm, wada=wada, win=win, wqr=qr, whd=hd,
                  wout=tiles(a["w_out"][0], KD), wwq=tiles(a["peer_wq"][0], KD), keys=keys, u=u_t, v=v_t)
    arrays = {k: np.ascontiguousarray(v) for k, v in arrays.items()}
    nc = bacc.Bacc("TRN2", target_bir_lowering=False, num_devices=1, dynamic_dma_scratch_size=1024)
    aps = [nc.dram_tensor(k, v.shape, mybir.dt.from_np(v.dtype), kind="ExternalInput").ap() for k, v in arrays.items()]
    out = nc.dram_tensor("out", [P, KD, T], F32, kind="ExternalOutput").ap()
    build(nc, *aps, out)
    r = run_bass_kernel_spmd(nc, [arrays], core_ids=[0])
    y = r.results[0]["out"]
    return y.transpose(1, 0, 2).reshape(D, T).T.reshape(1, T, D)
```

```python
from contextlib import ExitStack

import concourse.bass as bass
from concourse import mybir

F32 = mybir.dt.float32
F32R = mybir.dt.float32r
U32 = mybir.dt.uint32
I32 = mybir.dt.int32
BF16 = mybir.dt.bfloat16
ALU = mybir.AluOpType
ACT = mybir.ActivationFunctionType
AX_X = mybir.AxisListType.X

P = 128
T = 512
D = 2048
KD = D // P
TB = T // P
EPS = 1e-6
CONV_CH, CONV_W = 1024, 31
NC_T = CONV_CH // P
HEADS, NOPE, ROPE, VH = 8, 128, 64, 128
Q_LORA, KV_LORA = 768, 512
KQ, KKV = Q_LORA // P, KV_LORA // P
NLAT = KQ + KKV
SCALE = float(NOPE + ROPE) ** -0.5
PH_, TOPK, NKEY = 8, 16, 128
NEG = -3.0e38
CH = KD * P
W_HEAD = (KQ + KKV) * P

J_KR, J_LAT = 0, 1
J_CONV = J_LAT + NLAT
J_POOL = J_CONV + 2
J_QR = J_CONV + 2 * NC_T
J_VAL = J_QR + 2
J_HEAD = J_VAL + 2
J_OUT = J_HEAD + HEADS
J_WQ = J_OUT + KD
J_U = J_WQ + KD
J_V = J_U + NKEY

_cols = [("g1", KD), ("g2", KD), ("conv_b", NC_T), ("ln_g", NC_T), ("ln_b", NC_T), ("conv_w", NC_T * CONV_W),
         ("qa_g", KQ), ("kva_g", KKV), ("qn_g", 1), ("qr_g", 1), ("kn_g", 1), ("kr_g", 1),
         ("b_ada", 6 * KD), ("inv_freq", 1)]
COL, _n = {}, 0
for _name, _w in _cols:
    COL[_name] = (_n, _n + _w)
    _n += _w
NPRM = _n


LEAD, DMA_LEAD = 1, 16


class Tally:

    def __init__(self, eng, sem):
        self.eng, self.sem, self.base, self.turn, self.k = eng, sem, 0, None, 0

    def open(self, turn, per_turn):
        self.base += self.k
        self.turn, self.per, self.k = turn, per_turn, 0

    def close(self, turns):
        assert self.k == self.per, (self.k, self.per)
        self.base += self.per * turns
        self.turn, self.k = None, 0

    def mark(self, ins):
        ins.then_inc(self.sem, 1)
        self.k += 1
        return self.k

    def after(self, k):
        v = self.base + k
        self.eng.wait_ge(self.sem, v if self.turn is None else self.turn * self.per + v)

    def step(self, ins):
        self.after(self.mark(ins))


def build(nc, x_d, c_d, pos_d, prm_d, wada_d, win_d, wqr_d, wval_d, whd_d, wout_d, wwq_d, keys_d, u_d, v_d, out_d):
    gelu_d = nc.dram_tensor("gelu_scratch", [NKEY, P, T], F32).ap()
    gate_d = nc.dram_tensor("gate_scratch", [8, P, NKEY, 64], F32).ap()
    x1_d = nc.dram_tensor("x1_scratch", [P, KD, T], F32).ap()

    with ExitStack() as ctx:
        def at(name, kb, shape, dt=F32):
            return nc.alloc_sbuf_tensor_at(name, shape, dt, offset=1152 + int(kb * 1024))

        sems = {}

        def sem(name):
            if name not in sems:
                sems[name] = ctx.enter_context(nc.semaphore(name))
            return sems[name]

        bank = [ctx.enter_context(nc.psum_tensor(f"bank{i}", [P, T], F32)) for i in range(8)]

        act_hi = at("act_hi", 0, [P, KD, T], F32R)
        act_lo = at("act_lo", 32, [P, KD, T], F32R)
        att_o = at("att_o", 20, [P, HEADS, T])
        v_all = at("v_all", 20, [P, HEADS, T])
        sq_qr = at("sq_qr", 36, [P, 4, T])
        w_raw = [at(f"w_raw{s}", 64 + 8 * s, [P, CH]) for s in range(2)]
        w_hi = [at(f"w_hi{s}", 80 + 8 * s, [P, CH], F32R) for s in range(2)]
        w_lo = [at(f"w_lo{s}", 96 + 8 * s, [P, CH], F32R) for s in range(2)]
        X = at("X", 112, [P, KD, T])
        conv_o = at("conv_o", 112, [P, NC_T, T])
        sig = at("sig", 128, [P, T])
        glu = at("glu", 130, [P, CONV_W - 1 + T])
        tap_a = at("tap_a", 133, [P, T])
        tap_b = at("tap_b", 135, [P, T])
        conv_ws = at("conv_ws", 137, [P, CONV_W + 1])
        kr_rot = at("kr_rot", 138, [P, T])
        kr_sq = at("kr_sq", 140, [P, T])
        swapped = at("swapped", 142, [P, T])
        ada_w = [at(f"ada_w{s}", 144 + 8 * s, [P, D]) for s in range(4)]
        lat = at("lat", 160, [P, 1 + NLAT, T])
        c_all = at("c_all", 182, [P, D])
        sq = [at(f"sq{s}", 190 + 2 * s, [P, T]) for s in range(2)]
        qr_rot = at("qr_rot", 194, [P, 4, T])
        cos_t = at("cos_t", 204, [P, T])
        sin_t = at("sin_t", 206, [P, T])
        root = at("root", 208, [P, T])
        rstd = at("rstd", 210, [P, T])
        q_n = [at("q_n0", 128, [P, T]), at("q_n1", 190, [P, T])]
        k_n = [at("k_n0", 130, [P, T]), at("k_n1", 192, [P, T])]
        q_r = [at("q_r0", 132, [P, T]), at("q_r1", 202, [P, T])]
        k_r = [at("k_r0", 134, [P, T]), at("k_r1", 180, [P, T])]
        v_s = [at(f"v_s{s}", 160 + 2 * s, [P, T]) for s in range(2)]
        qk_root = [at(f"qk_root{s}", 136 + 6 * s, [P, T]) for s in range(2)]
        qk_rstd = [at("qk_rstd0", 204, [P, T]), at("qk_rstd1", 206, [P, T])]
        prob = [at(f"prob{s}", 164 + 2 * s, [P, T]) for s in range(2)]
        prob_t = at("prob_t", 168, [P, TB, T])
        sq_q = at("sq_q", 176, [P, T])
        sq_k = at("sq_k", 178, [P, T])
        flat_all = at("flat_all", 112, [P, TB, PH_, TOPK], U32)
        i1_all = at("i1_all", 114, [P, TB, PH_, TOPK], U32)
        i2_all = at("i2_all", 116, [P, TB, PH_, TOPK], U32)
        best_all = at("best_all", 118, [P, TB, PH_, TOPK])
        pick = at("pick", 120, [P, PH_, TOPK, TOPK])
        e1_t = at("e1_t", 128, [P, TB, P])
        e2_t = at("e2_t", 130, [P, TB, P])
        gate_t = at("gate_t", 132, [P, TB, P])
        part = at("part", 134, [P, P], U32)
        shifted = at("shifted", 134.5, [P, PH_, TOPK])
        expd = at("expd", 135, [P, PH_, TOPK])
        esum = at("esum", 135.5, [P, PH_])
        ersum = at("ersum", 135.75, [P, PH_])
        s_all = at("s_all", 120, [P, PH_, TB, 2 * NKEY])
        q_t = [at(f"q_t{s}", 168 + 2 * s, [P, T]) for s in range(2)]
        val = [at(f"val{s}", 172 + .25 * s, [P, TB, TOPK]) for s in range(2)]
        idx = [at(f"idx{s}", 172.5 + .25 * s, [P, TB, TOPK], U32) for s in range(2)]
        best = at("best", 173, [P, TB, TOPK])
        flat = at("flat", 173.25, [P, TB, TOPK], U32)
        s_left = [at(f"s_left{s}", 174 + .5 * s, [P, NKEY]) for s in range(2)]
        cand = at("cand", 175, [P, TOPK * TOPK])
        c_left = at("c_left", 176, [P, TOPK * TOPK])
        s_now = at("s_now", 177, [P, 2 * NKEY])
        keys = at("keys", 160, [P, PH_, 2, NKEY])
        g_chunk = [at(f"g_chunk{s}", 112 + 32 * s, [P, NKEY, 64]) for s in range(2)]
        hot2 = at("hot2", 176, [P, 16, P], BF16)
        hot1 = [at(f"hot1{j}", 180 + 4 * j, [P, 16, P], BF16) for j in range(3)]
        gelu_s = [at(f"gelu_s{s}", 200 + 2 * s, [P, T]) for s in range(2)]
        e1_c = at("e1_c", 204, [P, T], BF16)
        e2_c = at("e2_c", 205, [P, T], BF16)
        gate_c = [at(f"gate_c{j}", 206 + j, [P, T], BF16) for j in range(3)]
        iota_b = at("iota_b", 209, [P, P], BF16)
        gate_r = at("gate_r", 210, [P, T])
        wt_hi = [at(f"wt_hi{s}", 112 + 4 * s, [P, 2, T], F32R) for s in range(2)]
        wt_lo = [at(f"wt_lo{s}", 120 + 4 * s, [P, 2, T], F32R) for s in range(2)]
        wt = [at(f"wt{s}", 128 + 4 * s, [P, 2, T]) for s in range(2)]
        gelu_l = [at(f"gelu_l{s}", 136 + 4 * s, [P, 2, T]) for s in range(2)]
        gate_l2 = [at(f"gate_l2{s}", 144 + 4 * s, [P, 8, 2, 64]) for s in range(2)]
        x1_s = at("x1_s", 152, [P, 8, T])
        out_s = at("out_s", 168, [P, 8, T])
        prm = at("prm", 212, [P, NPRM])
        mod_raw = at("mod_raw", 214, [P, 6 * KD])
        mod = at("mod", 214.5, [P, 6 * KD])
        amp = at("amp", 215, [P, 2, KD])
        ones = at("ones", 215.25, [P, P])
        half = [at(f"half{s}", 215.75 + .5 * s, [P, P]) for s in range(2)]
        iota_i = at("iota_i", 216.75, [P, P], I32)
        iota_f = at("iota_f", 217.25, [P, P])
        ident = at("ident", 217.75, [P, P])
        tiny = at("tiny", 218.25, [P, 16])
        pos_i = at("pos_i", 219, [P, T], I32)
        eps_c, pidx, pidx_i = tiny[:, 0:1], tiny[:, 1:2], at("pidx_i", 218.5, [P, 1], I32)
        mx = [tiny[:, 2 + s:3 + s] for s in range(2)]
        nmx = [tiny[:, 4 + s:5 + s] for s in range(2)]
        rsum = [tiny[:, 6 + s:7 + s] for s in range(2)]
        rrec = [tiny[:, 8 + s:9 + s] for s in range(2)]
        hb = [bank[5], bank[6]]

        def pcol(name, i=0, n=1):
            a = COL[name][0] + i
            return prm[:, a:a + n]

        w_loaded = [sem(f"w_loaded{s}") for s in range(2)]
        hi_done, lo_done, lo_pool, pe_jobs = sem("hi_done"), sem("lo_done"), sem("lo_pool"), sem("pe_jobs")
        ada_loaded = [sem(f"ada_loaded{s}") for s in range(4)]
        ada_used = sem("ada_used")
        x_loaded, small_loaded, c_loaded, c_ready = sem("x_loaded"), sem("small_loaded"), sem("c_loaded"), sem("c_ready")
        const_ready, pool_chain = sem("const_ready"), sem("pool_chain")
        sq_ready, sq_used, sum_ready, root_ready, rstd_ready = (sem(n) for n in ("sq_ready", "sq_used", "sum_ready", "root_ready", "rstd_ready"))
        scaled, shifted_s, h_hi, h_lo = sem("scaled"), sem("shifted_s"), sem("h_hi"), sem("h_lo")
        angle_ready, trig_ready = sem("angle_ready"), sem("trig_ready")
        bank_used = [sem(f"bank_used{s}") for s in range(2)]
        lat_scaled, lat_hi, lat_lo = sem("lat_scaled"), sem("lat_hi"), sem("lat_lo")
        sig_ready, val_used, conv_done = sem("sig_ready"), sem("val_used"), sem("conv_done")
        rope_g, rope_sw, rope_done, rope_sq, qr_ready = (sem(n) for n in ("rope_g", "rope_sw", "rope_done", "rope_sq", "qr_ready"))
        q_ready, k_ready, q_used, k_used, v_copied = (sem(n) for n in ("q_ready", "k_ready", "q_used", "k_used", "v_copied"))
        v_set, v_ready, v_bank = sem("v_set"), sem("v_ready"), [bank[2], bank[3], bank[0], bank[1]]
        sqn_ready, ssq_ready, hroot_ready, hrstd_ready, qk_ready = (sem(n) for n in ("sqn_ready", "ssq_ready", "hroot_ready", "hrstd_ready", "qk_ready"))
        score_ready, max_ready, exp_ready, prob_ready, tr_ready, pt_ready, pv_ready, att_ready = (
            sem(n) for n in ("score_ready", "max_ready", "exp_ready", "prob_ready", "tr_ready", "pt_ready", "pv_ready", "att_ready"))
        mean_sum, mean_ready, centred, var_sum, ln_scaled, ln_silu, mix_hi, mix_lo = (
            sem(n) for n in ("mean_sum", "mean_ready", "centred", "var_sum", "ln_scaled", "ln_silu", "mix_hi", "mix_lo"))
        x2_loaded, x1_stored, keys_loaded = sem("x2_loaded"), sem("x1_stored"), sem("keys_loaded")
        qt_ready, sc_ready, sc_copied = sem("qt_ready"), sem("sc_ready"), sem("sc_copied")
        selected = sem("selected")
        gmax_ready, gexp_ready, tables_ready, tabt_ready, tabt_used = (sem(n) for n in ("gmax_ready", "gexp_ready", "tables_ready", "tabt_ready", "tabt_used"))
        gelu_ready = sem("gelu_ready")
        gelu_stored = [sem(f"gelu_stored{s}") for s in range(2)]
        hot_ready = [sem(f"hot_ready{s}") for s in range(4)]
        hot_used = [sem(f"hot_used{s}") for s in range(4)]
        g_copied = [sem(f"g_copied{s}") for s in range(2)]
        g_stored = [sem(f"g_stored{s}") for s in range(2)]
        wt_loaded = [sem(f"wt_loaded{s}") for s in range(2)]
        wt_ready = [sem(f"wt_ready{s}") for s in range(2)]
        wth_ready = [sem(f"wth_ready{s}") for s in range(2)]
        wtl_ready = [sem(f"wtl_ready{s}") for s in range(2)]
        y_sum, x1_loaded, y_ready, out_stored = sem("y_sum"), sem("x1_loaded"), sem("y_ready"), sem("out_stored")
        dve_chain, topk_chain = sem("dve_chain"), sem("topk_chain")

        def w_count(n0, turn=0):
            return 16 * (n0 // 2 + 1) + turn * 16

        def first_of_all(r, u, i):
            return isinstance(i, int) and u + i == 0

        def wait_lo(eng, n0, turn=0):
            if J_POOL <= n0 < J_HEAD:
                eng.wait_ge(lo_pool, n0 - J_POOL + 1 + turn * 2)
            else:
                eng.wait_ge(lo_done, n0 + 1 - (J_HEAD - J_POOL if n0 >= J_HEAD else 0) + turn * 2)

        block = ctx.enter_context(nc.Block())

        @block.sync
        def _(sp):
            def load_w(n0, src, width=CH, turn=0):
                if n0 >= 2:
                    wait_lo(sp, n0 - 2, turn)
                sp.dma_start(w_raw[n0 % 2][:, 0:width], src).then_inc(w_loaded[n0 % 2], 16)

            def load_ada(g0, slots, row, turn=0, per=0):
                if g0 >= slots:
                    sp.wait_ge(ada_used, g0 - slots + 1 + turn * per)
                s = g0 % slots
                sp.dma_start(ada_w[s][:], wada_d[row]).then_inc(ada_loaded[s], 16)

            sp.dma_start(c_all[:], c_d.partition_broadcast(P)).then_inc(c_loaded, 16)
            for s in range(4):
                load_ada(s, 4, s)
            sp.dma_start(X[:], x_d).then_inc(x_loaded, 16)
            load_w(0, win_d[0])
            load_w(1, win_d[1])
            with sp.Fori(0, 7) as i:
                for s in range(4):
                    load_ada(4 + s, 4, 4 + s + i * 4, i, 4)
            for m in range(2):
                load_ada(32 + m, 2, 32 + m)
            load_w(2, win_d[2])
            with sp.Fori(0, NLAT // 2) as i:
                for u in range(2):
                    for m in range(2):
                        load_ada(34 + 2 * u + m, 2, 34 + 2 * u + m + i * 4, i, 4)
                    load_w(3 + u, win_d[3 + u + i * 2], turn=i)
            for m in range(2):
                load_ada(54 + m, 2, 54 + m)
            for n in range(13, 15):
                load_w(n, win_d[n])
            with sp.Fori(0, NC_T - 2) as i:
                for u in range(2):
                    load_w(15 + u, win_d[15 + u + i * 2], turn=i)
            load_w(J_QR, wqr_d[0], KQ * 2 * P)
            load_w(J_QR + 1, wqr_d[1], KQ * 2 * P)
            load_w(J_VAL, wval_d[0])
            load_w(J_VAL + 1, wval_d[1])
            load_w(J_HEAD, whd_d[0], W_HEAD)
            load_w(J_HEAD + 1, whd_d[1], W_HEAD)
            load_ada(56, 2, 56)
            with sp.Fori(0, 3) as i:
                for u in range(2):
                    load_w(J_HEAD + 2 + u, whd_d[2 + u + i * 2], W_HEAD, turn=i)
                    load_ada(57 + u, 2, 57 + u + i * 2, i, 2)
            load_w(J_OUT, wout_d[0])
            load_ada(63, 2, 63)
            with sp.Fori(0, 7) as i:
                for u in range(2):
                    load_w(J_OUT + 1 + u, wout_d[1 + u + i * 2], turn=i)
                    load_ada(64 + u, 2, 64 + u + i * 2, i, 2)
            load_w(J_OUT + 15, wout_d[15])
            load_ada(78, 2, 78)
            load_w(J_WQ, wwq_d[0])
            load_ada(79, 2, 79)
            load_w(J_WQ + 1, wwq_d[1])
            with sp.Fori(0, 7) as i:
                for u in range(2):
                    load_w(J_WQ + 2 + u, wwq_d[2 + u + i * 2], turn=i)
            load_w(J_U, u_d[0])
            load_w(J_U + 1, u_d[1])
            for t0, t1 in ((0, 16), (16, 24), (24, 63)):
                with sp.Fori(t0, t1) as i:
                    for u in range(2):
                        load_w(J_U + 2 + u, u_d[2 + u + i * 2], turn=i)
                        if t0 == 16:
                            sp.wait_ge(selected, 1)
                            load_ada(48 + u, 2, 48 + u + i * 2, i, 2)
            def load_weights_of(u, turn, q_pass):
                rows = bass.ds(turn * 4 + 2 * u, 2)
                sp.wait_ge(wt_ready[u], LEAD + turn + 32 * q_pass)
                sp.dma_start(gelu_l[u][:], gelu_d[rows].rearrange("e p t -> p e t")).then_inc(wt_loaded[u], 16)
                sp.dma_start(gate_l2[u][:], gate_d[:, :, rows, :].rearrange("c p i t -> p c i t")).then_inc(wt_loaded[u], 16)

            for s in range(2):
                sp.wait_ge(g_stored[s], DMA_LEAD + 16 * 4)
                sp.wait_ge(gelu_stored[s], DMA_LEAD + 16 * 2)
            for u in range(2):
                load_weights_of(u, 0, 0)
            load_w(J_V, v_d[0])
            load_w(J_V + 1, v_d[1])
            for s in range(2):
                sp.wait_ge(gelu_stored[s], DMA_LEAD + 16 * NKEY // 2)
            for u in range(2):
                load_w(J_V + 2 + u, v_d[2 + u])
            for q_pass in range(2):
                with sp.Fori(1 - q_pass, 32 - q_pass) as i:
                    for u in range(2):
                        load_weights_of(u, i, q_pass)
                        load_w(J_V + 64 * q_pass + 2 + u, v_d[64 * q_pass + 2 + u + i * 2], turn=i)
            for u in range(2):
                load_weights_of(u, 31, 1)

        @block.gpsimd
        def _(pool):
            def done(ins, n):
                ins.then_inc(pool_chain, 1)
                pool.wait_ge(pool_chain, n)

            done(pool.iota(iota_i[:], pattern=[[1, P]], base=0, channel_multiplier=0), 1)
            done(pool.iota(pidx_i[:], pattern=[[0, 1]], base=0, channel_multiplier=1), 2)
            done(pool.memset(ones[:], 1.0), 3)
            done(pool.memset(eps_c, EPS), 4)
            for s in range(2):
                done(pool.memset(half[s][64 * s:64 * s + 64, :], 1.0), 5 + 2 * s)
                done(pool.memset(half[s][64 - 64 * s:128 - 64 * s, :], 0.0), 6 + 2 * s)
            pool.sem_inc(const_ready, 1)

            def low_h(which):
                for k in range(KD):
                    pool.wait_ge(h_hi, which * KD + k + 1)
                    pool.tensor_tensor(act_lo[:, k, :], X[:, k, :], act_hi[:, k, :].bitcast(F32), ALU.subtract).then_inc(h_lo, 1)

            def lo(n0, turn=0):
                pool.wait_ge(hi_done, n0 + 1 + turn * 2)
                s = n0 % 2
                pool.tensor_tensor(w_lo[s][:], w_raw[s][:], w_hi[s][:].bitcast(F32), ALU.subtract).then_inc(lo_pool, 1)

            low_h(0)
            with pool.Fori(0, NC_T - 1) as i:
                for n0 in (J_POOL, J_POOL + 1):
                    lo(n0, i)
            lo(J_QR)
            for k in range(NLAT):
                pool.wait_ge(lat_hi, k + 1)
                pool.tensor_tensor(act_lo[:, 6 + k, :], lat[:, 1 + k, :], act_hi[:, k, :].bitcast(F32), ALU.subtract).then_inc(lat_lo, 1)
            for n0 in range(J_QR + 1, J_HEAD):
                lo(n0)
            low_h(1)

        @block.scalar
        def _(act):
            def hi(n0, turn=0, width=CH):
                act.wait_ge(w_loaded[n0 % 2], w_count(n0, turn))
                if n0 >= 2:
                    act.wait_ge(pe_jobs, n0 - 1 + turn * 2)
                act.activation(w_hi[n0 % 2][:, 0:width], w_raw[n0 % 2][:, 0:width], ACT.Copy).then_inc(hi_done, 1)

            def squares(src, n, done0):
                for k in range(n):
                    if done0 + k >= 2:
                        act.wait_ge(sq_used, done0 + k - 1)
                    act.activation(sq[(done0 + k) % 2][:], src(k), ACT.Square).then_inc(sq_ready, 1)

            def modulate(which):
                for k in range(KD):
                    act.wait_ge(shifted_s, which * KD + k + 1)
                    act.activation(act_hi[:, k, :], X[:, k, :], ACT.Copy).then_inc(h_hi, 1)

            for q in (att_ready, sig_ready, exp_ready, qt_ready, sc_copied, *g_copied):
                act.sem_inc(q, LEAD)
            for q in (*gelu_stored, *g_stored):
                act.sem_inc(q, DMA_LEAD)
            act.dma_start(prm[:], prm_d).then_inc(small_loaded, 16)
            act.dma_start(pos_i[:], pos_d.partition_broadcast(P)).then_inc(small_loaded, 16)
            act.wait_ge(c_loaded, 16)
            act.activation(c_all[:], c_all[:], ACT.Silu).then_inc(c_ready, 1)
            act.wait_ge(const_ready, 1)
            act.wait_ge(x_loaded, 16)
            squares(lambda k: X[:, k, :], KD, 0)
            act.wait_ge(sum_ready, 1)
            act.activation(root[:], bank[2][:], ACT.Sqrt, bias=eps_c, scale=1.0 / D).then_inc(root_ready, 1)
            act.wait_ge(angle_ready, 1)
            act.activation(sin_t[:], sin_t[:], ACT.Sin).then_inc(trig_ready, 1)
            act.activation(cos_t[:], cos_t[:], ACT.Sin).then_inc(trig_ready, 1)
            hi(0)
            hi(1)
            modulate(0)

            def keep_latent(n0, turn=None):
                t = 0 if turn is None else turn
                act.wait_ge(pe_jobs, n0 + 1 + t * 2)
                act.activation(lat[:, n0 + t * 2, :] if turn is not None else lat[:, n0, :], bank[n0 % 2][:],
                               ACT.Copy).then_inc(bank_used[n0 % 2], 1)

            keep_latent(0)
            with act.Fori(0, NLAT // 2) as i:
                for u in range(2):
                    hi(J_LAT + 1 + u, i)
                    keep_latent(J_LAT + u, i)
            for s in range(2):
                act.wait_ge(bank_used[s], LEAD + BU_LAT_END[s])
            squares(lambda k: lat[:, 1 + k, :], NLAT, KD)
            act.activation(kr_sq[:], lat[:, 0, :], ACT.Square).then_inc(rope_sq, 1)
            hi(J_CONV + 1)
            act.wait_ge(sum_ready, 2)
            act.wait_ge(rstd_ready, 1)
            act.activation(root[:], bank[2][:], ACT.Sqrt, bias=eps_c, scale=1.0 / Q_LORA).then_inc(root_ready, 1)
            act.wait_ge(sum_ready, 3)
            act.wait_ge(rstd_ready, 2)
            act.activation(root[:], bank[3][:], ACT.Sqrt, bias=eps_c, scale=1.0 / KV_LORA).then_inc(root_ready, 1)

            def swap_halves(count):
                act.wait_ge(rope_g, count)
                for q in range(4):
                    src = tap_a[32 * (q ^ 1):32 * (q ^ 1) + 32, :]
                    act.activation(swapped[32 * q:32 * q + 32, :], src, ACT.Copy,
                                   scale=-1.0 if q % 2 == 0 else 1.0).then_inc(rope_sw, 1)

            def gate_channels(i):
                act.wait_ge(pe_jobs, J_CONV + 1 + i * 2)
                act.wait_ge(val_used, LEAD + i)
                act.activation(sig[:], bank[J_CONV % 2][:], ACT.Sigmoid).then_inc(sig_ready, 1)

            hi(J_CONV + 2)
            gate_channels(0)
            swap_halves(1)
            hi(J_CONV + 3)
            with act.Fori(1, NC_T - 1) as i:
                hi(J_CONV + 2, i)
                gate_channels(i)
                hi(J_CONV + 3, i)
            hi(J_QR)
            gate_channels(NC_T - 1)
            act.wait_ge(lat_scaled, NLAT)
            act.wait_ge(pe_jobs, J_QR)
            for k in range(NLAT):
                act.activation(act_hi[:, k, :], lat[:, 1 + k, :], ACT.Copy).then_inc(lat_hi, 1)
            hi(J_QR + 1)
            for t in range(4):
                act.wait_ge(qr_ready, t + 1)
                act.activation(sq_qr[:, t, :], bank[4 + t][:], ACT.Square).then_inc(rope_sq, 1)
                if t % 2 == 1:
                    hi(J_VAL + t // 2)
            for j in range(2):
                for tb in range(TB):
                    act.wait_ge(v_ready, 4 * j + tb + 1)
                    act.activation(v_all[:, 4 * j:4 * j + 4, tb * P:(tb + 1) * P], v_bank[tb][:].rearrange("p (h f) -> p h f", f=P),
                                   ACT.Copy).then_inc(v_copied, 1)
                    if j and tb % 2 == 0:
                        swap_halves(2 + tb // 2)
                hi(J_HEAD + j, width=W_HEAD)
            def square_of(r, u, i):
                act.wait_ge((q_ready, k_ready)[r], u + 1 + i * 2)
                if not first_of_all(r, u, i):
                    act.wait_ge(ssq_ready, 2 * u + r - 1 + i * 4)
                act.activation((sq_q, sq_k)[r][:], bank[r][:], ACT.Square).then_inc(sqn_ready, 1)

            def root_of(r, u, i):
                act.wait_ge(ssq_ready, 2 * u + r + 1 + i * 4)
                if not first_of_all(r, u, i):
                    act.wait_ge(hrstd_ready, 2 * u + r - 1 + i * 4)
                act.activation(qk_root[r][:], bank[2 + r][:], ACT.Sqrt, bias=eps_c,
                               scale=1.0 / (NOPE + ROPE)).then_inc(hroot_ready, 1)

            def exps(qb, u, i):
                w, s = (qb + 1) * P, qb % 2
                act.wait_ge(max_ready, 4 * u + qb + 1 + i * 8)
                if qb >= 2:
                    act.wait_ge(tr_ready, LEAD + 4 * u + qb - 1 + i * 8)
                else:
                    act.wait_ge(tr_ready, LEAD + 4 * u + i * 8)
                act.activation(prob[s][:, 0:w], hb[s][:, 0:w], ACT.Exp, bias=nmx[s], scale=SCALE,
                               accum_out=rsum[s]).then_inc(exp_ready, 1)

            def head(u, i, v=None, j=None, n_hi=None, turn=0, width=W_HEAD):
                exps(0, u, i)
                exps(1, u, i)
                if n_hi is not None:
                    hi(n_hi, turn, width)
                if v is not None:
                    square_of(0, v, j)
                exps(2, u, i)
                if v is not None:
                    square_of(1, v, j)
                exps(3, u, i)
                if v is not None:
                    root_of(0, v, j)
                act.wait_ge(tr_ready, LEAD + 4 * u + 4 + i * 8)
                act.activation(prob_t[:, :, 3 * P:4 * P], bank[7][:].rearrange("p (j q) -> p j q", q=P), ACT.Copy).then_inc(pt_ready, 1)
                if v is not None:
                    root_of(1, v, j)
                act.wait_ge(pv_ready, LEAD + u + 1 + i * 2)
                act.activation(att_o[:, u + i * 2, :], bank[4][:], ACT.Copy).then_inc(att_ready, 1)

            act.wait_ge(mean_sum, 1)
            act.activation(root[:], bank[3][:], ACT.Copy, scale=1.0 / CONV_CH).then_inc(mean_ready, 1)
            for r in range(2):
                swap_halves(4 + r)
                square_of(r, 0, 0)
            act.wait_ge(rope_done, 5)
            for r in range(2):
                root_of(r, 0, 0)
            for r in range(2):
                square_of(r, 1, 0)
            hi(J_HEAD + 2, width=W_HEAD)
            for k in range(NC_T):
                act.wait_ge(centred, k + 1)
                act.wait_ge(sq_used, KD + NLAT + k - 1)
                act.activation(sq[k % 2][:], conv_o[:, k, :], ACT.Square).then_inc(sq_ready, 1)
            act.wait_ge(var_sum, 1)
            act.activation(root[:], bank[2][:], ACT.Sqrt, bias=eps_c, scale=1.0 / CONV_CH).then_inc(root_ready, 1)
            for r in range(2):
                root_of(r, 1, 0)
            with act.Fori(0, 2) as i:
                for u in range(2):
                    head(u, i, u, i + 1, J_HEAD + 3 + u, i)
            head(0, 2, 0, 3, J_HEAD + 7)
            head(1, 2, 1, 3, J_OUT, 0, CH)
            head(0, 3, n_hi=J_OUT + 1, width=CH)
            head(1, 3)

            def load_x(k0, k1):
                act.dma_start(X[:, k0:k1, :], x_d[:, k0:k1, :]).then_inc(x2_loaded, 16)

            act.wait_ge(att_ready, LEAD + HEADS)
            load_x(8, KD)
            for k in range(HEADS):
                if k >= 2:
                    act.wait_ge(mix_lo, k - 1)
                act.activation(act_hi[:, NC_T + k, :], att_o[:, k, :], ACT.Copy).then_inc(mix_hi, 1)
            for k in range(NC_T):
                act.wait_ge(ln_scaled, k + 1)
                act.activation(conv_o[:, k, :], conv_o[:, k, :], ACT.Silu, bias=pcol("ln_b", k),
                               scale=pcol("ln_g", k)).then_inc(ln_silu, 1)
                act.wait_ge(ln_silu, k + 1)
                act.activation(act_hi[:, k, :], conv_o[:, k, :], ACT.Copy).then_inc(mix_hi, 1)
                if k == 5:
                    act.wait_ge(mix_lo, HEADS + 4)
                    load_x(0, 4)
            act.dma_start(keys[:], keys_d).then_inc(keys_loaded, 16)
            act.wait_ge(mix_lo, 2 * NC_T)
            load_x(4, 8)
            def store_x1(k0, turn=None):
                b = (J_OUT + k0) % 2
                t = 0 if turn is None else turn
                act.wait_ge(bank_used[b], LEAD + BU_OUT0[b] + k0 // 2 + 1 + t)
                act.dma_start(x1_d[:, bass.ds(k0 + t * 2, 1), :] if turn is not None else x1_d[:, k0:k0 + 1, :],
                              X[:, bass.ds(k0 + t * 2, 1), :] if turn is not None else X[:, k0:k0 + 1, :]).then_inc(x1_stored, 16)

            with act.Fori(0, 7) as i:
                for u in range(2):
                    hi(J_OUT + 2 + u, i)
                    store_x1(u, i)
            hi(J_OUT + 16)
            store_x1(14)
            store_x1(15)

            act.wait_ge(sum_ready, 4)
            act.activation(root[:], bank[2][:], ACT.Sqrt, bias=eps_c, scale=1.0 / D).then_inc(root_ready, 1)
            modulate(1)
            hi(J_WQ + 1)

            def keep_query(half_i, h):
                act.wait_ge(pe_jobs, J_WQ + 1 + half_i + h * 2)
                act.activation(q_t[half_i][:], bank[(J_WQ + half_i) % 2][:], ACT.Copy).then_inc(qt_ready, 1)
                hi(J_WQ + 2 + half_i, h)

            def keep_scores(h):
                for g in range(2):
                    act.wait_ge(sc_ready, LEAD + h * 2 + g + 1)
                    act.activation(s_all[:, h, 2 * g:2 * g + 2, :], bank[2 + g][:].rearrange("p (b n) -> p b n", b=2),
                                   ACT.Copy).then_inc(sc_copied, 1)

            keep_query(0, 0)
            keep_query(1, 0)
            with act.Fori(0, PH_ - 1) as h:
                act.wait_ge(sc_ready, LEAD + 2 + h * 2)
                keep_query(0, h + 1)
                keep_scores(h)
                keep_query(1, h + 1)
            keep_scores(PH_ - 1)

            def gelu_job(u, turn):
                hi(J_U + 2 + u, turn)
                act.wait_ge(gelu_stored[u], DMA_LEAD + turn * 16)
                act.activation(gelu_s[u][:], bank[(J_U + u) % 2][:], ACT.Gelu_apprx_tanh).then_inc(bank_used[(J_U + u) % 2], 1)

            def gelu_store(u, turn):
                b = (J_U + u) % 2
                act.wait_ge(bank_used[b], LEAD + BU_U0[b] + 1 + turn)
                act.dma_start(gelu_d[turn * 2 + u], gelu_s[u][:]).then_inc(gelu_stored[u], 16)

            with act.Fori(0, 16) as i:
                for u in range(2):
                    gelu_job(u, i)
                    gelu_store(u, i)
            with act.Fori(0, TB) as b:
                act.wait_ge(gmax_ready, 1 + b)
                act.activation(expd[:], shifted[:], ACT.Exp).then_inc(gexp_ready, 1)
                for half_turn in range(2):
                    for u in range(2):
                        gelu_job(u, 16 + half_turn + b * 2)
                        gelu_store(u, 16 + half_turn + b * 2)
            for u in range(2):
                gelu_job(u, 24)
                gelu_store(u, 24)
            with act.Fori(0, 4) as c:
                for cb in range(2):
                    act.wait_ge(g_stored[cb], DMA_LEAD + c * 16)
                    with act.Fori(0, 4) as b:
                        turn = c * 8 + (4 * cb) + b
                        for u in range(2):
                            gelu_job(u, turn + 25)
                            gelu_store(u, turn + 25)
                            for g in range(2):
                                act.wait_ge(hot_used[2 * u + g], LEAD + turn + 1)
                                act.activation(g_chunk[cb][:, :, bass.ds(b * 16 + (8 * u + 4 * g), 4)],
                                               bank[2 + g][:].rearrange("p (t i) -> p i t", t=4),
                                               ACT.Copy).then_inc(g_copied[g], 1)
                    for g in range(2):
                        act.wait_ge(g_copied[g], LEAD + c * 16 + 8 * cb + 8)
                    act.dma_start(gate_d[c * 2 + cb], g_chunk[cb][:]).then_inc(g_stored[cb], 16)
            with act.Fori(57, 63) as i:
                for u in range(2):
                    gelu_job(u, i)
                    gelu_store(u, i)

            for s in range(2):
                act.wait_ge(g_stored[s], DMA_LEAD + 16 * 4)
            act.wait_ge(hot_used[3], LEAD + 32)
            act.dma_start(x1_s[:], x1_d[:, 0:8, :]).then_inc(x1_loaded, 16)

            def weigh_hi(u, turn):
                act.wait_ge(wt_ready[u], LEAD + turn + 1)
                act.activation(wt_hi[u][:], wt[u][:], ACT.Copy).then_inc(wth_ready[u], 1)

            weigh_hi(0, 0)
            weigh_hi(1, 0)
            for u in range(2):
                gelu_job(u, 63)
                gelu_store(u, 63)
            for q_pass in range(2):
                with act.Fori(0, 32 - q_pass) as i:
                    for u in range(2):
                        hi(J_V + 64 * q_pass + 2 + u, i)
                        weigh_hi(u, i + 1 + 32 * q_pass)
                for d in range(0, 8, 2):
                    k = 8 * q_pass + d
                    act.wait_ge(y_ready, k + 2)
                    act.dma_start(out_d[:, k:k + 2, :], out_s[:, d:d + 2, :]).then_inc(out_stored, 16)
                if q_pass == 0:
                    act.dma_start(x1_s[:], x1_d[:, 8:16, :]).then_inc(x1_loaded, 16)
            act.wait_ge(out_stored, 2 * 4 * 16)

        @block.vector
        def _(dve):
            T_ = Tally(dve, dve_chain)

            def lo(n0, turn=0, width=CH):
                dve.wait_ge(hi_done, n0 + 1 + turn * 2)
                s = n0 % 2
                dve.tensor_tensor(w_lo[s][:, 0:width], w_raw[s][:, 0:width], w_hi[s][:, 0:width].bitcast(F32),
                                  ALU.subtract).then_inc(lo_done, 1)

            def ada(g0, slots, count, col, turn=0):
                s = g0 % slots
                dve.wait_ge(ada_loaded[s], 16 * count + turn * 16)
                dve.scalar_tensor_tensor(out=ada_w[s][:], in0=ada_w[s][:], scalar=1.0, in1=c_all[:], op0=ALU.mult,
                                         op1=ALU.mult, accum_out=col).then_inc(ada_used, 1)

            def ada_mid(m0, turn=0, per=0):
                g0 = 32 + m0
                col = mod_raw[:, bass.ds(turn * per + g0, 1)] if per else mod_raw[:, g0:g0 + 1]
                s = g0 % 2
                dve.wait_ge(ada_loaded[s], 16 * (8 + m0 // 2 + 1) + (turn * (8 * per) if per else 0))
                dve.scalar_tensor_tensor(out=ada_w[s][:], in0=ada_w[s][:], scalar=1.0, in1=c_all[:], op0=ALU.mult,
                                         op1=ALU.mult, accum_out=col).then_inc(ada_used, 1)

            for q in (val_used, pt_ready, *wt_ready):
                dve.sem_inc(q, LEAD)
            dve.wait_ge(const_ready, 1)
            T_.mark(dve.tensor_copy(iota_f[:], iota_i[:]))
            T_.step(dve.tensor_copy(pidx, pidx_i[:]))
            T_.step(dve.tensor_scalar(ident[:], iota_f[:], pidx, None, ALU.is_equal))

            dve.wait_ge(c_ready, 1)
            def ada_rounds(r0, r1):
                with dve.Fori(r0, r1) as i:
                    for s in range(4):
                        ada(s, 4, 1, mod_raw[:, bass.ds(i * 4 + s, 1)], i)

            ada_rounds(0, 4)
            dve.wait_ge(small_loaded, 32)
            PI = 3.1415925
            C1, C2 = 6.28125, 0.0019350051879882812
            C3 = 6.283185307179586 - C1 - C2
            MAGIC = 12582912.0
            ang, turns_ = qr_rot[:, 0, :], qr_rot[:, 1, :]
            T_.step(dve.tensor_copy(ang, pos_i[:]))
            T_.step(dve.tensor_scalar(ang, ang, pcol("inv_freq"), None, ALU.mult))
            T_.step(dve.tensor_scalar(turns_, ang, 1.0 / 6.283185307179586, MAGIC, ALU.mult, ALU.add))
            T_.step(dve.tensor_scalar(turns_, turns_, -MAGIC, None, ALU.add))
            for cc in (C1, C2, C3):
                T_.step(dve.scalar_tensor_tensor(out=ang, in0=turns_, scalar=-cc, in1=ang, op0=ALU.mult, op1=ALU.add))
            T_.step(dve.tensor_scalar(cos_t[:], ang, 1.5707963267948966, None, ALU.add))
            T_.step(dve.tensor_scalar(turns_, cos_t[:], PI, -6.283185307179586, ALU.is_gt, ALU.mult))
            T_.step(dve.tensor_tensor(cos_t[:], cos_t[:], turns_, ALU.add))
            T_.step(dve.tensor_scalar(cos_t[:], cos_t[:], PI, -PI, ALU.min, ALU.max))
            dve.tensor_scalar(sin_t[:], ang, PI, -PI, ALU.min, ALU.max).then_inc(angle_ready, 1)
            dve.wait_ge(angle_ready, 1)

            lo(0)
            lo(1)
            ada_rounds(4, 7)
            dve.wait_ge(root_ready, 1)
            dve.reciprocal(rstd[:], root[:]).then_inc(rstd_ready, 1)
            dve.wait_ge(rstd_ready, 1)
            ada_rounds(7, 8)
            dve.wait_ge(ada_used, 32)
            T_.step(dve.tensor_tensor(mod[:, 0:32], mod_raw[:, 0:32], pcol("b_ada", 0, 32), ALU.add))
            T_.step(dve.scalar_tensor_tensor(out=amp[:, 0, :], in0=mod[:, KD:2 * KD], scalar=1.0,
                                             in1=pcol("g1", 0, KD), op0=ALU.add, op1=ALU.mult))

            def modulate(which):
                def shift(k):
                    dve.wait_ge(scaled, which * KD + k + 1)
                    m = 3 * which * KD + k
                    dve.tensor_scalar(X[:, k, :], X[:, k, :], mod[:, m:m + 1], None, ALU.add).then_inc(shifted_s, 1)

                for k in range(KD):
                    if k >= 1:
                        shift(k - 1)
                    dve.scalar_tensor_tensor(out=X[:, k, :], in0=X[:, k, :], scalar=amp[:, which, k:k + 1],
                                             in1=rstd[:], op0=ALU.mult, op1=ALU.mult).then_inc(scaled, 1)
                shift(KD - 1)

            modulate(0)
            for m in range(2):
                ada_mid(m)
            with dve.Fori(0, NLAT // 2) as i:
                for u in range(2):
                    lo(J_LAT + 1 + u, i)
                    for m in range(2):
                        ada_mid(2 + 2 * u + m, i, 4)
            lo(J_CONV + 1)
            for r, (a, n, g) in enumerate(((1, KQ, "qa_g"), (1 + KQ, KKV, "kva_g"))):
                dve.wait_ge(root_ready, 2 + r)
                if r:
                    dve.wait_ge(lat_scaled, KQ)
                dve.reciprocal(rstd[:], root[:]).then_inc(rstd_ready, 1)
                dve.wait_ge(rstd_ready, 2 + r)
                for k in range(n):
                    dve.scalar_tensor_tensor(out=lat[:, a + k, :], in0=lat[:, a + k, :], scalar=pcol(g, k),
                                             in1=rstd[:], op0=ALU.mult, op1=ALU.mult).then_inc(lat_scaled, 1)

            def rope(src, gain, out, count):
                dve.tensor_scalar(tap_a[:], src, gain, None, ALU.mult).then_inc(rope_g, 1)
                dve.wait_ge(rope_g, count)
                T_.mark(dve.tensor_tensor(tap_b[:], tap_a[:], cos_t[:], ALU.mult))
                dve.wait_ge(rope_sw, 4 * count)
                T_.step(dve.tensor_tensor(swapped[:], swapped[:], sin_t[:], ALU.mult))
                dve.tensor_tensor(out, tap_b[:], swapped[:], ALU.add).then_inc(rope_done, 1)
                dve.wait_ge(rope_done, count)

            dve.wait_ge(trig_ready, 2)
            rope(lat[:, 0, :], pcol("kr_g"), kr_rot[:], 1)
            T_.step(dve.memset(glu[:, 0:CONV_W - 1], 0.0))
            with dve.Fori(0, NC_T) as i:
                T_.open(i, 3 + CONV_W)
                k1 = T_.mark(dve.tensor_copy(conv_ws[:, 0:CONV_W], prm[:, bass.ds(i * CONV_W + COL["conv_w"][0], CONV_W)]))
                k2 = T_.mark(dve.tensor_copy(conv_ws[:, CONV_W:CONV_W + 1], prm[:, bass.ds(i + COL["conv_b"][0], 1)]))
                dve.wait_ge(sig_ready, LEAD + i + 1)
                dve.wait_ge(pe_jobs, J_CONV + 2 + i * 2)
                dve.tensor_tensor(glu[:, CONV_W - 1:], bank[(J_CONV + 1) % 2][:], sig[:], ALU.mult).then_inc(val_used, 1)
                dve.wait_ge(val_used, LEAD + i + 1)
                T_.after(k2)
                acc, last = [tap_a, tap_b], [0, 0]
                for k in range(CONV_W):
                    w = conv_ws[:, k:k + 1]
                    src = glu[:, k:k + T]
                    a = k % 2
                    if k >= 2:
                        T_.after(last[a])
                    if k == 0:
                        ins = dve.tensor_scalar(tap_a[:], src, w, conv_ws[:, CONV_W:CONV_W + 1], ALU.mult, ALU.add)
                    elif k == 1:
                        ins = dve.tensor_scalar(tap_b[:], src, w, None, ALU.mult)
                    else:
                        ins = dve.scalar_tensor_tensor(out=acc[a][:], in0=src, scalar=w, in1=acc[a][:], op0=ALU.mult, op1=ALU.add)
                    last[a] = T_.mark(ins)
                T_.after(max(last))
                T_.step(dve.tensor_tensor(conv_o[:, i, :], tap_a[:], tap_b[:], ALU.add))
                T_.close(NC_T)
            dve.sem_inc(conv_done, 1)

            for m in range(2):
                ada_mid(22 + m)
            for t in range(4):
                if t % 2 == 0:
                    lo(J_HEAD + t // 2, width=W_HEAD)
                dve.wait_ge(rope_sq, 2 + t)
                rope(bank[4 + t][:], pcol("qr_g"), qr_rot[:, t, :], 2 + t)

            def norm_of(r, u, i):
                r0, r1 = 64 * u, 64 * u + 64
                dve.wait_ge(hroot_ready, 2 * u + r + 1 + i * 4)
                if not (isinstance(i, int) and u + i == 0):
                    dve.wait_ge(qk_ready, u + i * 2)
                dve.reciprocal(qk_rstd[r][:], qk_root[r][:]).then_inc(hrstd_ready, 1)
                dve.wait_ge(hrstd_ready, 2 * u + r + 1 + i * 4)
                dve.scalar_tensor_tensor(out=(q_n, k_n)[r][u][:], in0=bank[r][:], scalar=pcol(("qn_g", "kn_g")[r]), in1=qk_rstd[r][:],
                                         op0=ALU.mult, op1=ALU.mult).then_inc((q_used, k_used)[r], 1)
                if r == 0:
                    T_.step(dve.tensor_tensor(q_r[u][r0:r1, :], qr_rot[r0:r1, i, :], qk_rstd[0][r0:r1, :], ALU.mult))
                    dve.wait_ge(q_used, u + 1 + i * 2)
                else:
                    dve.tensor_tensor(k_r[u][r0:r1, :], kr_rot[r0:r1, :], qk_rstd[1][r0:r1, :], ALU.mult).then_inc(qk_ready, 1)

            def row_max(qb, u, i):
                w, s = (qb + 1) * P, qb % 2
                dve.wait_ge(score_ready, 4 * u + qb + 1 + i * 8)
                T_.step(dve.memset(hb[s][0:64, w - 64:w], NEG))
                T_.step(dve.reduce_max(mx[s], hb[s][:, 0:w], AX_X))
                dve.tensor_scalar(nmx[s], mx[s], -SCALE, None, ALU.mult).then_inc(max_ready, 1)

            def normalise(qb, u, i):
                w, s = (qb + 1) * P, qb % 2
                dve.wait_ge(exp_ready, LEAD + 4 * u + qb + 1 + i * 8)
                T_.step(dve.reciprocal(rrec[s], rsum[s]))
                dve.tensor_scalar(prob[s][:, 0:w], prob[s][:, 0:w], rrec[s], None, ALU.mult).then_inc(prob_ready, 1)

            def keep_t(qb, u, i):
                w = (qb + 1) * P
                if qb == 0:
                    dve.wait_ge(pv_ready, LEAD + u + i * 2)
                dve.wait_ge(tr_ready, LEAD + 4 * u + qb + 1 + i * 8)
                dve.tensor_copy(prob_t[:, 0:qb + 1, qb * P:qb * P + P],
                                bank[7][:, 0:w].rearrange("p (j q) -> p j q", q=P)).then_inc(pt_ready, 1)

            def head(u, i, k_of=None, q_of=None, beside=None):
                row_max(0, u, i)
                row_max(1, u, i)
                dve.tensor_copy(v_s[u][:], v_all[:, u + i * 2, :]).then_inc(v_set, 1)
                normalise(0, u, i)
                if k_of:
                    norm_of(1, *k_of)
                keep_t(0, u, i)
                row_max(2, u, i)
                normalise(1, u, i)
                if beside:
                    beside()
                keep_t(1, u, i)
                row_max(3, u, i)
                normalise(2, u, i)
                keep_t(2, u, i)
                normalise(3, u, i)
                if q_of:
                    norm_of(0, *q_of)

            NORM, SOFT = 1, 12
            norm_of(0, 0, 0)
            norm_of(1, 0, 0)
            dve.wait_ge(mean_ready, 1)
            for k in range(NC_T):
                dve.tensor_tensor(conv_o[:, k, :], conv_o[:, k, :], root[:], ALU.subtract).then_inc(centred, 1)
            norm_of(0, 1, 0)
            ada_mid(24)
            lo(J_HEAD + 2, width=W_HEAD)
            with dve.Fori(0, 2) as i:
                T_.open(i, 2 * NORM + 2 * SOFT)
                for u in range(2):
                    head(u, i, (1 - u, i + u), (u, i + 1), lambda: (lo(J_HEAD + 3 + u, i, W_HEAD), ada_mid(25 + u, i, 2)))
                T_.close(2)
            head(0, 2, (1, 2), (0, 3), lambda: (lo(J_HEAD + 7, width=W_HEAD), ada_mid(29)))
            head(1, 2, (0, 3), (1, 3), lambda: (lo(J_OUT), ada_mid(30)))
            def ln_scale(k0):
                for k in range(k0, k0 + 4):
                    dve.tensor_tensor(conv_o[:, k, :], conv_o[:, k, :], rstd[:], ALU.mult).then_inc(ln_scaled, 1)

            head(0, 3, (1, 3), None, lambda: (ada_mid(31), lo(J_OUT + 1)))
            dve.wait_ge(root_ready, 4)
            dve.wait_ge(centred, NC_T)
            dve.reciprocal(rstd[:], root[:]).then_inc(rstd_ready, 1)
            dve.wait_ge(rstd_ready, 4)
            head(1, 3, None, None, lambda: ln_scale(0))
            ln_scale(4)
            dve.wait_ge(ada_used, 64)
            T_.step(dve.tensor_tensor(mod[:, 32:64], mod_raw[:, 32:64], pcol("b_ada", 32, 32), ALU.add))

            for k in range(HEADS):
                dve.wait_ge(mix_hi, k + 1)
                dve.tensor_tensor(act_lo[:, NC_T + k, :], att_o[:, k, :], act_hi[:, NC_T + k, :].bitcast(F32),
                                  ALU.subtract).then_inc(mix_lo, 1)
            dve.wait_ge(mix_lo, HEADS)
            for k in range(NC_T):
                dve.wait_ge(mix_hi, HEADS + k + 1)
                dve.tensor_tensor(act_lo[:, k, :], conv_o[:, k, :], act_hi[:, k, :].bitcast(F32), ALU.subtract).then_inc(mix_lo, 1)

            def residual(m, n0, turn=None):
                b = n0 % 2
                t = 0 if turn is None else turn
                dve.wait_ge(pe_jobs, n0 + 1 + t * 2)
                col = mod[:, bass.ds(t * 2 + 2 * KD + m, 1)] if turn is not None else mod[:, 2 * KD + m:2 * KD + m + 1]
                xt = X[:, m + t * 2, :] if turn is not None else X[:, m, :]
                dve.scalar_tensor_tensor(out=xt, in0=bank[b][:], scalar=col, in1=xt, op0=ALU.mult,
                                         op1=ALU.add).then_inc(bank_used[b], 1)
                dve.wait_ge(bank_used[b], LEAD + BU_OUT0[b] + m // 2 + 1 + t)
                dve.wait_ge(sq_used, SQ_OUT + m - 1 + t * 2)
                dve.tensor_tensor(sq[m % 2][:], xt, xt, ALU.mult).then_inc(sq_ready, 1)

            dve.wait_ge(x2_loaded, 3 * 16)
            with dve.Fori(0, 7) as i:
                for u in range(2):
                    lo(J_OUT + 2 + u, i)
                    residual(u, J_OUT + u, i)
                    ada_mid(32 + u, i, 2)
            lo(J_OUT + 16)
            residual(14, J_OUT + 14)
            ada_mid(46)
            residual(15, J_OUT + 15)
            ada_mid(47)
            dve.wait_ge(ada_used, 80)
            T_.step(dve.tensor_tensor(mod[:, 64:80], mod_raw[:, 64:80], pcol("b_ada", 64, 16), ALU.add))
            T_.step(dve.scalar_tensor_tensor(out=amp[:, 1, :], in0=mod[:, 4 * KD:5 * KD], scalar=1.0,
                                             in1=pcol("g2", 0, KD), op0=ALU.add, op1=ALU.mult))

            dve.wait_ge(root_ready, 5)
            dve.reciprocal(rstd[:], root[:]).then_inc(rstd_ready, 1)
            dve.wait_ge(rstd_ready, 5)
            dve.wait_ge(x1_stored, 16 * KD)
            modulate(1)
            lo(J_WQ + 1)

            K_ = Tally(dve, topk_chain)

            def top16(jobs):
                a = [K_.mark(dve.max(v[:, 0:8], s)) for v, ix, s, left in jobs]
                b = []
                for (v, ix, s, left), k in zip(jobs, a):
                    K_.after(k)
                    b.append(K_.mark(dve.match_replace(left, v[:, 0:8], s, NEG)))
                c_ = [K_.mark(dve.max_index(ix[:, 0:8], v[:, 0:8], s)) for v, ix, s, left in jobs]
                d_ = []
                for (v, ix, s, left), k in zip(jobs, b):
                    K_.after(k)
                    d_.append(K_.mark(dve.max(v[:, 8:16], left)))
                for (v, ix, s, left), k in zip(jobs, d_):
                    K_.after(k)
                    e_ = K_.mark(dve.max_index(ix[:, 8:16], v[:, 8:16], left))
                return e_

            def select(b, h):
                S = s_now
                K_.step(dve.tensor_copy(s_now[:], s_all[:, h, b, :]))
                v1, v2 = val[0][:, b, :], val[1][:, b, :]
                K_.after(top16([(v1, idx[0][:, b, :], S[:, 0:NKEY], s_left[0][:]),
                                (v2, idx[1][:, b, :], S[:, NKEY:2 * NKEY], s_left[1][:])]))
                K_.step(dve.tensor_tensor(cand[:].rearrange("p (a b) -> p a b", b=TOPK), v1.unsqueeze(2).broadcast_to([P, TOPK, TOPK]),
                                  v2.unsqueeze(1).broadcast_to([P, TOPK, TOPK]), ALU.add))
                return top16([(best[:, b, :], flat[:, b, :], cand[:], c_left[:])])

            with dve.Fori(0, PH_) as h:
                for u in range(2):
                    lo(J_WQ + 2 + u, h)

            dve.wait_ge(sc_copied, LEAD + 2 * PH_)
            with dve.Fori(0, PH_) as h:
                dve.sem_clear(topk_chain)
                K_.k = 0
                for b in range(TB):
                    lo(J_U + 2 + b, h * 2)
                    K_.after(select(b, h))
                K_.mark(dve.tensor_copy(flat_all[:, :, h, :], flat[:]))
                K_.mark(dve.tensor_copy(i1_all[:, :, h, :], idx[0][:]))
                K_.mark(dve.tensor_copy(i2_all[:, :, h, :], idx[1][:]))
                K_.step(dve.tensor_copy(best_all[:, :, h, :], best[:]))

            dve.sem_inc(selected, 1)
            hot16 = iota_f[:, 0:TOPK].unsqueeze(1).broadcast_to([P, P, TOPK])

            with dve.Fori(0, TB) as b:
                T_.open(b, 11)
                fl = flat_all[:, b, :, :].rearrange("p h k -> p (h k)")
                bs = best_all[:, b, :, :]
                dve.tensor_tensor(shifted[:], bs, bs[:, :, 0:1].broadcast_to([P, PH_, TOPK]), ALU.subtract).then_inc(gmax_ready, 1)
                for half_i, (tab, ia, op, arg) in enumerate(((e1_t, i1_all, ALU.logical_shift_right, 4), (e2_t, i2_all, ALU.bitwise_and, 15))):
                    lo(J_U + 34 + 2 * half_i, b * 2)
                    ada_mid(48 + 2 * half_i, b, 4)
                    T_.step(dve.tensor_scalar(part[:], fl, arg, None, op))
                    T_.step(dve.tensor_tensor(pick[:].rearrange("p h k a -> p (h k) a"),
                                              part[:].unsqueeze(2).broadcast_to([P, P, TOPK]), hot16, ALU.is_equal))
                    lo(J_U + 35 + 2 * half_i, b * 2)
                    ada_mid(49 + 2 * half_i, b, 4)
                    T_.step(dve.tensor_tensor(pick[:], pick[:], ia[:, b, :, :].unsqueeze(2).broadcast_to([P, PH_, TOPK, TOPK]), ALU.mult))
                    T_.step(dve.tensor_reduce(tab[:, b, :], pick[:].rearrange("p h k a -> p (h k) a"), AX_X, ALU.add))
                dve.wait_ge(gexp_ready, 1 + b)
                T_.step(dve.reduce_sum(esum[:], expd[:], AX_X))
                T_.step(dve.reciprocal(ersum[:], esum[:]))
                T_.step(dve.tensor_tensor(gate_t[:, b, :].rearrange("p (h k) -> p h k", h=PH_), expd[:],
                                          ersum[:].unsqueeze(2).broadcast_to([P, PH_, TOPK]), ALU.mult))
                T_.close(TB)
            dve.sem_inc(tables_ready, 1)
            lo(J_U + 50)
            dve.wait_ge(tabt_ready, 3)
            T_.mark(dve.tensor_copy(e1_c[:], bank[2][:]))
            T_.mark(dve.tensor_copy(e2_c[:], bank[3][:]))
            T_.mark(dve.tensor_copy(iota_b[:], iota_f[:]))
            T_.step(dve.tensor_copy(gate_c[0][:], bank[4][:]))
            T_.step(dve.tensor_tensor(gate_r[:], bank[4][:], gate_c[0][:], ALU.subtract))
            T_.step(dve.tensor_copy(gate_c[1][:], gate_r[:]))
            T_.step(dve.tensor_tensor(gate_c[2][:], gate_r[:], gate_c[1][:], ALU.subtract))
            dve.sem_inc(tabt_used, 1)

            dve.wait_ge(ada_used, 96)
            T_.step(dve.tensor_tensor(mod[:, 80:96], mod_raw[:, 80:96], pcol("b_ada", 80, 16), ALU.add))

            lo(J_U + 51)
            with dve.Fori(0, 32) as i:
                for u in range(2):
                    for g in range(2):
                        dve.wait_ge(hot_used[2 * u + g], LEAD + i)
                        for q in range(4):
                            r = 8 * u + 4 * g + q
                            tok = bass.ds(i * 16 + r, 1)
                            dve.tensor_scalar(hot2[:, r, :], iota_b[:], e2_c[:, tok], None, ALU.is_equal)
                            for j in range(3):
                                ins = dve.tensor_scalar(hot1[j][:, r, :], iota_b[:], e1_c[:, tok], gate_c[j][:, tok],
                                                        ALU.is_equal, ALU.mult)
                        ins.then_inc(hot_ready[2 * u + g], 1)
                    lo(J_U + 52 + u, i)

            def weigh(u, turn):
                dve.wait_ge(wt_loaded[u], (turn + 1) * 32)
                dve.tensor_tensor(wt[u][:].rearrange("p i (c t) -> p i c t", c=8), gelu_l[u][:].rearrange("p i (c t) -> p i c t", c=8),
                                  gate_l2[u][:].rearrange("p c i t -> p i c t"), ALU.mult).then_inc(wt_ready[u], 1)

            def weigh_lo(u, turn):
                dve.wait_ge(wth_ready[u], turn + 1)
                dve.tensor_tensor(wt_lo[u][:], wt[u][:], wt_hi[u][:].bitcast(F32), ALU.subtract).then_inc(wtl_ready[u], 1)

            with dve.Fori(57, 63) as i:
                for u in range(2):
                    lo(J_U + 2 + u, i)
            for u in range(2):
                weigh(u, 0)
            for u in range(2):
                weigh_lo(u, 0)
            for u in range(2):
                lo(J_V + u)
            for q_pass in range(2):
                def prepare(u, i):
                    lo(J_V + 64 * q_pass + 2 + u, i)
                    weigh(u, i + 1 + 32 * q_pass)
                    weigh_lo(u, i + 1 + 32 * q_pass)

                with dve.Fori(0, 31) as i:
                    for u in range(2):
                        prepare(u, i)
                if q_pass == 0:
                    prepare(0, 31)
                dve.wait_ge(x1_loaded, 16 * (q_pass + 1))
                if q_pass:
                    dve.wait_ge(out_stored, 4 * 16)
                for d in range(8):
                    dve.wait_ge(y_sum, 8 * q_pass + d + 1)
                    m = 5 * KD + 8 * q_pass + d
                    dve.scalar_tensor_tensor(out=out_s[:, d, :], in0=bank[d][:], scalar=mod[:, m:m + 1], in1=x1_s[:, d, :],
                                             op0=ALU.mult, op1=ALU.add).then_inc(y_ready, 1)
                if q_pass == 0:
                    prepare(1, 31)

        @block.tensor
        def _(pe):
            def dense(slot, out, nk, koff, hi_t, lo_t, before=None):
                for k in range(nk):
                    if before:
                        before(k)
                    wh = w_hi[slot][:, koff + k * P:koff + (k + 1) * P]
                    wl = w_lo[slot][:, koff + k * P:koff + (k + 1) * P]
                    pe.matmul(out, wh, hi_t(k), start=(k == 0), stop=False)
                    pe.matmul(out, wh, lo_t(k), start=False, stop=False)
                    last = pe.matmul(out, wl, hi_t(k), start=False, stop=(k == nk - 1))
                return last

            H = lambda k: act_hi[:, k, :]
            L = lambda k: act_lo[:, k, :]

            def job(n0, turn=0, used=None, before=None, hi_t=H, lo_t=L):
                wait_lo(pe, n0, turn)
                if used is not None:
                    pe.wait_ge(*used)
                dense(n0 % 2, bank[n0 % 2][:], KD, 0, hi_t, lo_t, before).then_inc(pe_jobs, 1)

            def sums(n, out, done0):
                for k in range(n):
                    pe.wait_ge(sq_ready, done0 + k + 1)
                    last = pe.matmul(out[:], ones[:], sq[(done0 + k) % 2][:], start=(k == 0), stop=(k == n - 1))
                    if k < n - 1:
                        last.then_inc(sq_used, 1)
                last.then_inc(sq_used, 1)
                pe.wait_ge(sq_used, done0 + n)
                pe.sem_inc(sum_ready, 1)

            for q in (tr_ready, pv_ready, sc_ready, *hot_used, *bank_used):
                pe.sem_inc(q, LEAD)
            pe.wait_ge(const_ready, 1)
            sums(KD, bank[2], 0)
            job(0, before=lambda k: pe.wait_ge(h_lo, k + 1))
            with pe.Fori(0, NLAT // 2) as i:
                job(1, i, (bank_used[1], LEAD + i))
                job(2, i, (bank_used[0], LEAD + i + 1))
            sums(KQ, bank[2], KD)
            sums(KKV, bank[3], KD + KQ)
            for s in range(2):
                pe.wait_ge(bank_used[s], LEAD + BU_LAT_END[s])
            job(J_CONV)
            job(J_CONV + 1)
            with pe.Fori(0, NC_T - 1) as i:
                job(J_CONV + 2, i, (sig_ready, LEAD + 1 + i))
                job(J_CONV + 3, i, (val_used, LEAD + 1 + i))
            LL = lambda k: act_lo[:, 6 + k, :]
            for j in range(2):
                wait_lo(pe, J_QR + j)
                for t in range(2):
                    last = dense((J_QR + j) % 2, bank[4 + 2 * j + t][:], KQ, t * KQ * P, H, LL,
                                 (lambda k: pe.wait_ge(lat_lo, k + 1)) if j + t == 0 else None)
                    last.then_inc(qr_ready, 1)
                pe.wait_ge(qr_ready, 2 * j + 2)
                pe.sem_inc(pe_jobs, 1)
            pe.wait_ge(lat_lo, NLAT)

            for j in range(2):
                s = (J_VAL + j) % 2
                wait_lo(pe, J_VAL + j)
                for tb in range(TB):
                    tk = slice(tb * P, tb * P + P)
                    if j:
                        pe.wait_ge(v_copied, tb + 1)
                    elif tb == 2:
                        pe.wait_ge(val_used, LEAD + NC_T)
                        pe.wait_ge(sig_ready, LEAD + NC_T)
                    for k in range(KKV):
                        ah, al = act_hi[:, KQ + k, tk], act_lo[:, 6 + KQ + k, tk]
                        wv = slice(k * 4 * P, (k + 1) * 4 * P)
                        pe.matmul(v_bank[tb][:], ah, w_hi[s][:, wv], start=(k == 0), stop=False)
                        pe.matmul(v_bank[tb][:], al, w_hi[s][:, wv], start=False, stop=False)
                        last = pe.matmul(v_bank[tb][:], ah, w_lo[s][:, wv], start=False, stop=(k == KKV - 1))
                    last.then_inc(v_ready, 1)
                pe.wait_ge(v_ready, 4 * j + 4)
                pe.sem_inc(pe_jobs, 1)
            pe.wait_ge(v_copied, 2 * TB)
            pe.wait_ge(conv_done, 1)
            for k in range(NC_T):
                last = pe.matmul(bank[3][:], ones[:], conv_o[:, k, :], start=(k == 0), stop=(k == NC_T - 1))
            last.then_inc(mean_sum, 1)

            def project(r, u, i):
                s = (J_HEAD + u) % 2
                if r == 0:
                    wait_lo(pe, J_HEAD + u, i)
                    pe.wait_ge(q_used, u + i * 2)
                    dense(s, bank[0][:], KQ, 0, H, LL).then_inc(q_ready, 1)
                else:
                    pe.wait_ge(k_used, u + i * 2)
                    dense(s, bank[1][:], KKV, KQ * P, lambda k: act_hi[:, KQ + k, :],
                          lambda k: act_lo[:, 6 + KQ + k, :]).then_inc(k_ready, 1)
                    pe.wait_ge(k_ready, u + 1 + i * 2)
                    pe.sem_inc(pe_jobs, 1)

            def sum_squares(r, u, i):
                pe.wait_ge(sqn_ready, 2 * u + r + 1 + i * 4)
                if not first_of_all(r, u, i):
                    pe.wait_ge(hroot_ready, 2 * u + r - 1 + i * 4)
                pe.matmul(bank[2 + r][:], ones[:], (sq_q, sq_k)[r][:], start=True, stop=False)
                if r == 0:
                    last = pe.matmul(bank[2][:], half[u][:], sq_qr[:, i, :], start=False, stop=True)
                else:
                    last = pe.matmul(bank[3][:], half[0][:], kr_sq[:], start=False, stop=True)
                last.then_inc(ssq_ready, 1)

            def score(qb, u, i):
                r0, r1 = 64 * u, 64 * u + 64
                w, qs = (qb + 1) * P, slice(qb * P, qb * P + P)
                if qb == 0:
                    pe.wait_ge(qk_ready, u + 1 + i * 2)
                if qb >= 2:
                    pe.wait_ge(exp_ready, LEAD + 4 * u + qb - 1 + i * 8)
                elif qb == 0:
                    pe.wait_ge(exp_ready, LEAD + 4 * u + i * 8)
                o = hb[qb % 2][:, 0:w]
                pe.matmul(o, q_n[u][:, qs], k_n[u][:, 0:w], start=True, stop=False)
                pe.matmul(o, q_r[u][r0:r1, qs], k_r[u][r0:r1, 0:w], start=False, stop=True).then_inc(score_ready, 1)

            def turn_probs(qb, u, i):
                pe.wait_ge(prob_ready, 4 * u + qb + 1 + i * 8)
                pe.wait_ge(pt_ready, LEAD + 4 * u + qb + i * 8)
                for j in range(qb + 1):
                    last = pe.transpose(bank[7][:, j * P:(j + 1) * P], prob[qb % 2][:, j * P:(j + 1) * P], ident[:])
                last.then_inc(tr_ready, 1)

            def weigh_values(u, i):
                pe.wait_ge(pt_ready, LEAD + 4 * u + 4 + i * 8)
                pe.wait_ge(att_ready, LEAD + u + i * 2)
                pe.wait_ge(v_set, u + 1 + i * 2)
                for j in range(TB):
                    last = pe.matmul(bank[4][:, j * P:], v_s[u][:, j * P:(j + 1) * P], prob_t[:, j, j * P:],
                                     start=(j == 0), stop=(j == TB - 1))
                last.then_inc(pv_ready, 1)

            def head(u, i, v=None, j=None):
                score(0, u, i)
                score(1, u, i)
                if v is not None:
                    project(0, v, j)
                turn_probs(0, u, i)
                score(2, u, i)
                if v is not None:
                    project(1, v, j)
                    sum_squares(0, v, j)
                turn_probs(1, u, i)
                score(3, u, i)
                if v is not None:
                    sum_squares(1, v, j)
                turn_probs(2, u, i)
                turn_probs(3, u, i)
                weigh_values(u, i)

            for r in range(2):
                project(r, 0, 0)
            pe.wait_ge(mean_ready, 1)
            for r in range(2):
                sum_squares(r, 0, 0)
            for r in range(2):
                project(r, 1, 0)
            pe.wait_ge(hroot_ready, 1)
            for k in range(NC_T):
                pe.wait_ge(sq_ready, KD + NLAT + k + 1)
                last = pe.matmul(bank[2][:], ones[:], sq[k % 2][:], start=(k == 0), stop=(k == NC_T - 1))
                last.then_inc(sq_used, 1)
            pe.wait_ge(sq_used, KD + NLAT + NC_T)
            pe.sem_inc(var_sum, 1)
            pe.wait_ge(root_ready, 4)
            for r in range(2):
                sum_squares(r, 1, 0)
            pe.wait_ge(rope_sq, 5)
            pe.wait_ge(rope_done, 5)
            with pe.Fori(0, 3) as i:
                for u in range(2):
                    head(u, i, u, i + 1)
            head(0, 3)
            head(1, 3)

            order = list(range(NC_T, KD)) + list(range(NC_T))

            def out_job(n0, turn=0, used=None, first=False):
                s = n0 % 2
                wait_lo(pe, n0, turn)
                if used:
                    pe.wait_ge(*used)
                for at_, k in enumerate(order):
                    if first:
                        pe.wait_ge(mix_lo, at_ + 1)
                    wh, wl = w_hi[s][:, k * P:(k + 1) * P], w_lo[s][:, k * P:(k + 1) * P]
                    pe.matmul(bank[s][:], wh, act_hi[:, k, :], start=(at_ == 0), stop=False)
                    pe.matmul(bank[s][:], wh, act_lo[:, k, :], start=False, stop=False)
                    last = pe.matmul(bank[s][:], wl, act_hi[:, k, :], start=False, stop=(at_ == KD - 1))
                last.then_inc(pe_jobs, 1)

            def add_squares(k0, turn=0, start=False, stop=False):
                pe.wait_ge(sq_ready, SQ_OUT + k0 + 1 + turn * 2)
                pe.matmul(bank[2][:], ones[:], sq[k0 % 2][:], start=start, stop=stop).then_inc(sq_used, 1)

            out_job(J_OUT, first=True)
            out_job(J_OUT + 1)
            pe.wait_ge(hroot_ready, 2 * HEADS)
            add_squares(0, start=True)
            with pe.Fori(0, 7) as i:
                for u in range(2):
                    b = (J_OUT + u) % 2
                    out_job(J_OUT + 2 + u, i, (bank_used[b], LEAD + i + BU_OUT0[b] + 1))
                    add_squares(1 + u, i)
            add_squares(15, stop=True)
            for s in range(2):
                pe.wait_ge(bank_used[s], LEAD + BU_OUT_END[s])
            pe.wait_ge(sq_used, SQ_OUT + KD)
            pe.sem_inc(sum_ready, 1)

            def scores(h):
                pe.wait_ge(qt_ready, LEAD + 2 + h * 2)
                for g in range(2):
                    pe.wait_ge(sc_copied, LEAD + h * 2)
                    for b in (2 * g, 2 * g + 1):
                        for half_i in range(2):
                            at_ = ((b % 2) * 2 + half_i) * NKEY
                            last = pe.matmul(bank[2 + g][:, at_:at_ + NKEY], q_t[half_i][:, b * P:b * P + P],
                                             keys[:, h, half_i, :], start=True, stop=True)
                    last.then_inc(sc_ready, 1)

            pe.wait_ge(keys_loaded, 16)
            job(J_WQ, before=lambda k: pe.wait_ge(h_lo, KD + k + 1))
            job(J_WQ + 1)
            with pe.Fori(0, PH_ - 1) as h:
                job(J_WQ + 2, h, (qt_ready, LEAD + 1 + h * 2))
                scores(h)
                job(J_WQ + 3, h, (qt_ready, LEAD + 2 + h * 2))
            scores(PH_ - 1)

            pe.wait_ge(qt_ready, LEAD + 2 * PH_)

            def u_job(u, turn):
                b = (J_U + u) % 2
                job(J_U + u, turn, (bank_used[b], LEAD + turn + BU_U0[b]))

            with pe.Fori(0, 24) as i:
                for u in range(2):
                    u_job(u, i)
            u_job(0, 24)
            pe.wait_ge(tables_ready, 1)
            pe.wait_ge(sc_copied, LEAD + 2 * PH_)
            for t_i, tab in enumerate((e1_t, e2_t, gate_t)):
                for b in range(TB):
                    last = pe.transpose(bank[2 + t_i][:, b * P:(b + 1) * P], tab[:, b, :], ident[:])
                last.then_inc(tabt_ready, 1)
            u_job(1, 24)
            pe.wait_ge(tabt_used, 1)
            with pe.Fori(0, 32) as i:
                for u in range(2):
                    u_job(u, i + 25)
                    for g in range(2):
                        pe.wait_ge(hot_ready[2 * u + g], i + 1)
                        pe.wait_ge(g_copied[g], LEAD + i * 2 + u)
                        for q in range(4):
                            s = 8 * u + 4 * g + q
                            o = bank[2 + g][:, q * P:(q + 1) * P]
                            for j in range(3):
                                last = pe.matmul(o, hot2[:, s, :], hot1[j][:, s, :], start=(j == 0), stop=(j == 2))
                        last.then_inc(hot_used[2 * u + g], 1)

            with pe.Fori(57, 64) as i:
                for u in range(2):
                    u_job(u, i)

            for s in range(2):
                pe.wait_ge(bank_used[s], LEAD + BU_U_END[s])
                pe.wait_ge(g_copied[s], LEAD + 64)

            def v_job(q_pass, u, turn, start=False, stop=False):
                n0 = J_V + 64 * q_pass + u
                s = n0 % 2
                wait_lo(pe, n0, turn)
                pe.wait_ge(wtl_ready[u], turn + 1 + 32 * q_pass)
                for e in range(2):
                    for d in range(8):
                        if start and e == 0 and q_pass:
                            pe.wait_ge(y_ready, d + 1)
                        col = slice(e * 1024 + d * P, e * 1024 + (d + 1) * P)
                        pe.matmul(bank[d][:], w_hi[s][:, col], wt_hi[u][:, e, :], start=(start and e == 0), stop=False)
                        pe.matmul(bank[d][:], w_hi[s][:, col], wt_lo[u][:, e, :], start=False, stop=False)
                        last = pe.matmul(bank[d][:], w_lo[s][:, col], wt_hi[u][:, e, :], start=False, stop=(stop and e == 1))
                        if stop and e == 1:
                            last.then_inc(y_sum, 1)
                if stop:
                    pe.wait_ge(y_sum, 8 * (q_pass + 1))
                    pe.sem_inc(pe_jobs, 1)
                else:
                    last.then_inc(pe_jobs, 1)

            for q_pass in range(2):
                v_job(q_pass, 0, 0, start=True)
                v_job(q_pass, 1, 0)
                with pe.Fori(1, 31) as i:
                    for u in range(2):
                        v_job(q_pass, u, i)
                v_job(q_pass, 0, 31)
                v_job(q_pass, 1, 31, stop=True)


SQ_OUT = KD + NLAT + NC_T
BU_LAT_END = [6, 5]
BU_OUT0 = [6, 5]
BU_OUT_END = [BU_OUT0[0] + 8, BU_OUT0[1] + 8]
BU_U0 = BU_OUT_END
BU_U_END = [BU_U0[0] + 64, BU_U0[1] + 64]


def kernel(**inputs):
    import numpy as np
    import concourse.bacc as bacc
    from concourse.bass_utils import run_bass_kernel_spmd

    a = {k: np.asarray(v) for k, v in inputs.items()}

    def tiles(w, n_out):
        k = w.shape[0] // P
        return w.reshape(k, P, n_out, P).transpose(2, 1, 0, 3).reshape(n_out, P, k * P)

    def cols(v):
        return v.reshape(-1, P).T

    w_in = a["w_in"][0]
    o1 = 2 * CONV_CH
    conv_pairs = np.stack([w_in[:, CONV_CH:o1].reshape(D, NC_T, P), w_in[:, :CONV_CH].reshape(D, NC_T, P)], 2).reshape(D, o1)
    kr = w_in[:, o1 + Q_LORA + KV_LORA:]
    win = tiles(np.concatenate([kr, kr, w_in[:, o1:o1 + Q_LORA + KV_LORA], conv_pairs], 1), 1 + NLAT + 2 * NC_T)
    uq = a["w_uq"][0].reshape(Q_LORA, HEADS, NOPE + ROPE)
    ukv = a["w_ukv"][0].reshape(KV_LORA, HEADS, NOPE + VH)
    qr = tiles(uq[:, :, NOPE:].reshape(Q_LORA, 4 * P), 4).reshape(2, 2, P, KQ * P).transpose(0, 2, 1, 3).reshape(2, P, 2 * KQ * P)
    val = ukv[:, :, NOPE:].reshape(KKV, P, 2, 4 * P).transpose(2, 1, 0, 3).reshape(2, P, CH)
    hd = np.concatenate([tiles(uq[:, :, :NOPE].reshape(Q_LORA, -1), HEADS), tiles(ukv[:, :, :NOPE].reshape(KV_LORA, -1), HEADS)], 2)
    keys = np.stack([a["peer_k1"][0], a["peer_k2"][0]], 1).transpose(3, 0, 1, 2)
    u_t = a["peer_u"][0].reshape(NKEY, P, KD, P).transpose(0, 3, 2, 1).reshape(NKEY, P, CH)
    v_t = a["peer_v"][0].reshape(64, 2, P, 2, 1024).transpose(3, 0, 2, 1, 4).reshape(NKEY, P, CH)
    wada = a["w_ada"][0].T.reshape(6 * KD, P, D)
    conv_w = a["conv_dw_w"][0].reshape(CONV_W, NC_T, P).transpose(2, 1, 0).reshape(P, NC_T * CONV_W)
    inv = (10000.0 ** (-np.arange(0, ROPE, 2, dtype=np.float32) / ROPE)).astype(np.float32)
    qg, kg = a["q_norm_g"][0], a["k_norm_g"][0]
    two = lambda v: np.concatenate([v, v])[:, None]
    prm = np.concatenate([cols(a["norm1_g"][0]), cols(a["norm2_g"][0]), cols(a["conv_dw_b"][0]), cols(a["conv_ln_g"][0]),
                          cols(a["conv_ln_b"][0]), conv_w, cols(a["q_a_norm_g"][0]), cols(a["kv_a_norm_g"][0]),
                          qg[:NOPE, None], two(qg[NOPE:]), kg[:NOPE, None], two(kg[NOPE:]), cols(a["b_ada"][0]),
                          np.tile(inv, 4)[:, None]], 1)
    x_t = a["x"][0].T.reshape(KD, P, T).transpose(1, 0, 2)
    arrays = dict(x=x_t, c=a["c"].reshape(D), pos=a["positions"].reshape(T), prm=prm, wada=wada, win=win, wqr=qr, wval=val, whd=hd,
                  wout=tiles(a["w_out"][0], KD), wwq=tiles(a["peer_wq"][0], KD), keys=keys, u=u_t, v=v_t)
    arrays = {k: np.ascontiguousarray(v) for k, v in arrays.items()}
    nc = bacc.Bacc("TRN2", target_bir_lowering=False, num_devices=1, dynamic_dma_scratch_size=1024)
    aps = [nc.dram_tensor(k, v.shape, mybir.dt.from_np(v.dtype), kind="ExternalInput").ap() for k, v in arrays.items()]
    out = nc.dram_tensor("out", [P, KD, T], F32, kind="ExternalOutput").ap()
    build(nc, *aps, out)
    r = run_bass_kernel_spmd(nc, [arrays], core_ids=[0])
    y = r.results[0]["out"]
    return y.transpose(1, 0, 2).reshape(D, T).T.reshape(1, T, D)
```
